# Optimizing a Trainium2 kernel written in Bass

```python
import math
import jax
import jax.numpy as jnp
from jax import lax
import numpy as np

D_MODEL = 1024
BATCH = 1
SEQ = 512
DEPTH = 2

HEAD_DIM = 64
A_Q_HEADS = 8
A_KV_HEADS = 2
A_RADIUS = 128
B_HEADS = 4
B_V_DIM = 2 * HEAD_DIM
C_PATTERNS = ((128, 1), (512, 4), (2048, 16))
C_HEADS = 8
D_HEADS = 8
D_Q_RANK = 384
D_KV_RANK = 256
D_NOPE = 64
D_ROPE = 32
D_V = 64
ROPE_THETA = 10000.0
N_BRANCH = 4
BRANCH_WIDTH = 512
D_FF = 2816
CONV_WIDTH = 3
Q_BLOCK = 128
EPS = 1e-6
NEG = -1e30
IN_SPLITS = (
    A_Q_HEADS * HEAD_DIM,
    A_KV_HEADS * HEAD_DIM,
    A_KV_HEADS * HEAD_DIM,
    2 * B_HEADS * HEAD_DIM,
    2 * B_HEADS * HEAD_DIM,
    B_HEADS * B_V_DIM,
    3 * len(C_PATTERNS) * C_HEADS * HEAD_DIM,
    D_Q_RANK,
    D_KV_RANK,
    D_ROPE,
    N_BRANCH * D_MODEL,
)
N_IN = sum(IN_SPLITS)

kernel_name = "hybrid_gated_parallel_attn_encoder"

def _split_points(sizes):
    pts, acc = [], 0
    for n in sizes[:-1]:
        acc += n
        pts.append(acc)
    return pts

def rms_norm(x, g):
    xf = x.astype(jnp.float32)
    y = xf * lax.rsqrt(jnp.mean(xf * xf, axis=-1, keepdims=True) + EPS) * g.astype(jnp.float32)
    return y.astype(x.dtype)

def alibi_slopes(n):
    return jnp.asarray(2.0 ** (-8.0 * np.arange(1, n + 1) / n), jnp.float32)

def rope(t, pos):
    half = t.shape[-1] // 2
    inv = ROPE_THETA ** (-jnp.arange(half, dtype=jnp.float32) / half)
    ang = pos.astype(jnp.float32)[:, :, None, None] * inv
    c, sn = jnp.cos(ang), jnp.sin(ang)
    t1 = t[..., :half].astype(jnp.float32)
    t2 = t[..., half:].astype(jnp.float32)
    return jnp.concatenate([t1 * c - t2 * sn, t1 * sn + t2 * c], axis=-1).astype(t.dtype)

def banded_attention(q, k, v, pos, radius, slopes, sink=None):
    n, length, kh, g, d = q.shape
    blk = radius
    nb = -(-length // blk)
    pad = nb * blk - length

    def padl(t):
        return jnp.pad(t, [(0, 0), (0, pad)] + [(0, 0)] * (t.ndim - 2))

    def windows(t):
        tb = t.reshape((n, nb, blk) + t.shape[2:])
        tp = jnp.pad(tb, [(0, 0), (1, 1)] + [(0, 0)] * (tb.ndim - 2))
        return jnp.concatenate([tp[:, :-2], tp[:, 1:-1], tp[:, 2:]], axis=2)

    valid = jnp.broadcast_to(jnp.arange(nb * blk) < length, (n, nb * blk))
    qb = padl(q).reshape(n, nb, blk, kh, g, d)
    kw, vw = windows(padl(k)), windows(padl(v))
    posf = padl(pos).astype(jnp.float32)
    pw, vwin = windows(posf), windows(valid)
    s = jnp.einsum('nbqkgd,nbskd->nbkgqs', qb, kw, preferred_element_type=jnp.float32) * (d ** -0.5)
    dist = jnp.abs(posf.reshape(n, nb, blk)[..., :, None] - pw[..., None, :])
    s = s - slopes[None, None, :, :, None, None] * dist[:, :, None, None]
    rel = (jnp.arange(3 * blk) - blk)[None, :] - jnp.arange(blk)[:, None]
    mask = (jnp.abs(rel) <= radius)[None, None] & vwin[:, :, None, :]
    s = jnp.where(mask[:, :, None, None], s, NEG)
    m = jnp.max(s, axis=-1)
    if sink is not None:
        sk = sink.astype(jnp.float32)[None, None, :, :, None]
        m = jnp.maximum(m, sk)
    p = jnp.exp(s - m[..., None])
    den = jnp.sum(p, axis=-1)
    if sink is not None:
        den = den + jnp.exp(sk - m)
    o = jnp.einsum('nbkgqs,nbskv->nbqkgv', p.astype(v.dtype), vw, preferred_element_type=jnp.float32)
    o = o / jnp.transpose(den, (0, 1, 4, 2, 3))[..., None]
    lse = jnp.transpose(m + jnp.log(den), (0, 1, 4, 2, 3))
    o = o.reshape(n, nb * blk, kh, g, -1)[:, :length]
    lse = lse.reshape(n, nb * blk, kh, g)[:, :length]
    return o.astype(q.dtype), lse

def windowed_gqa(a_q, a_k, a_v, pos, q_norm, k_norm, sink):
    b, s, _ = a_q.shape
    grp = A_Q_HEADS // A_KV_HEADS
    q = rms_norm(a_q.reshape(b, s, A_KV_HEADS, grp, HEAD_DIM), q_norm)
    k = rms_norm(a_k.reshape(b, s, A_KV_HEADS, HEAD_DIM), k_norm)
    v = a_v.reshape(b, s, A_KV_HEADS, HEAD_DIM)
    slopes = alibi_slopes(A_Q_HEADS).reshape(A_KV_HEADS, grp)
    o, _ = banded_attention(q, k, v, pos, A_RADIUS, slopes, sink.reshape(A_KV_HEADS, grp))
    return o.reshape(b, s, A_Q_HEADS * HEAD_DIM)

def differential_attention(b_q, b_k, b_v, pos, q_norm, k_norm, lam_q1, lam_k1, lam_q2, lam_k2, subln_g, lam_init):
    b, s, _ = b_q.shape
    q = rms_norm(b_q.reshape(b, s, 2, B_HEADS, HEAD_DIM), q_norm)
    k = rms_norm(b_k.reshape(b, s, 2, B_HEADS, HEAD_DIM), k_norm)
    v = b_v.reshape(b, s, B_HEADS, B_V_DIM)
    lam = (jnp.exp(jnp.sum(lam_q1 * lam_k1, -1).astype(jnp.float32))
           - jnp.exp(jnp.sum(lam_q2 * lam_k2, -1).astype(jnp.float32)) + lam_init)
    slopes = alibi_slopes(B_HEADS)
    nb = s // Q_BLOCK
    posf = pos.astype(jnp.float32)
    qb = jnp.moveaxis(q.reshape(b, nb, Q_BLOCK, 2, B_HEADS, HEAD_DIM), 1, 0)
    pb = jnp.moveaxis(posf.reshape(b, nb, Q_BLOCK), 1, 0)
    scale = HEAD_DIM ** -0.5

    def block(args):
        qblk, pblk = args
        sc = jnp.einsum('bqmhd,bsmhd->bmhqs', qblk, k, preferred_element_type=jnp.float32) * scale
        dist = jnp.abs(pblk[:, :, None] - posf[:, None, :])
        sc = sc - slopes[None, None, :, None, None] * dist[:, None, None]
        a = jax.nn.softmax(sc, axis=-1)
        a = a[:, 0] - lam[None, :, None, None] * a[:, 1]
        return jnp.einsum('bhqs,bshv->bqhv', a.astype(v.dtype), v, preferred_element_type=jnp.float32)

    o = lax.map(block, (qb, pb))
    o = jnp.moveaxis(o, 0, 1).reshape(b, s, B_HEADS, B_V_DIM)
    o = rms_norm(o, subln_g) * (1.0 - lam_init)
    return o.reshape(b, s, B_HEADS * B_V_DIM).astype(b_v.dtype)

def dilated_attention(c_qkv, pos, q_norm, k_norm):
    b, s, _ = c_qkv.shape
    ng = len(C_PATTERNS)
    per = c_qkv.reshape(b, s, ng, 3, C_HEADS, HEAD_DIM)
    slopes = alibi_slopes(ng * C_HEADS).reshape(ng, C_HEADS)
    outs, lses = [], []
    for j, (window, r) in enumerate(C_PATTERNS):
        def strided(t):
            t = t.reshape((b, s // r, r) + t.shape[2:])
            t = jnp.moveaxis(t, 2, 1)
            return t.reshape((b * r, s // r) + t.shape[3:])

        def unstrided(t):
            t = t.reshape((b, r, s // r) + t.shape[2:])
            t = jnp.moveaxis(t, 1, 2)
            return t.reshape((b, s) + t.shape[3:])

        q = rms_norm(per[:, :, j, 0], q_norm)
        k = rms_norm(per[:, :, j, 1], k_norm)
        v = per[:, :, j, 2]
        o, lse = banded_attention(strided(q)[:, :, :, None], strided(k), strided(v), strided(pos),
                                  window // (2 * r), slopes[j][:, None])
        outs.append(unstrided(o[:, :, :, 0]))
        lses.append(unstrided(lse[:, :, :, 0]))
    w = jax.nn.softmax(jnp.stack(lses, 0), axis=0)
    o = jnp.sum(w[..., None] * jnp.stack(outs, 0).astype(jnp.float32), axis=0)
    return o.reshape(b, s, C_HEADS * HEAD_DIM).astype(c_qkv.dtype)

def latent_attention(d_cq, d_ckv, d_kr, pos, cq_norm, ckv_norm, w_uq, w_ukv, q_norm, k_norm):
    b, s, _ = d_cq.shape
    q = (rms_norm(d_cq, cq_norm) @ w_uq).reshape(b, s, D_HEADS, D_NOPE + D_ROPE)
    kv = (rms_norm(d_ckv, ckv_norm) @ w_ukv).reshape(b, s, D_HEADS, D_NOPE + D_V)
    k = jnp.concatenate([kv[..., :D_NOPE], jnp.broadcast_to(d_kr[:, :, None, :], (b, s, D_HEADS, D_ROPE))], axis=-1)
    v = kv[..., D_NOPE:]
    q = rms_norm(q, q_norm)
    k = rms_norm(k, k_norm)
    q = jnp.concatenate([q[..., :D_NOPE], rope(q[..., D_NOPE:], pos)], axis=-1)
    k = jnp.concatenate([k[..., :D_NOPE], rope(k[..., D_NOPE:], pos)], axis=-1)
    nb = s // Q_BLOCK
    qb = jnp.moveaxis(q.reshape(b, nb, Q_BLOCK, D_HEADS, D_NOPE + D_ROPE), 1, 0)
    scale = (D_NOPE + D_ROPE) ** -0.5

    def block(qblk):
        sc = jnp.einsum('bqhd,bshd->bhqs', qblk, k, preferred_element_type=jnp.float32) * scale
        a = jax.nn.softmax(sc, axis=-1)
        return jnp.einsum('bhqs,bshv->bqhv', a.astype(v.dtype), v, preferred_element_type=jnp.float32)

    o = jnp.moveaxis(lax.map(block, qb), 0, 1)
    return o.reshape(b, s, D_HEADS * D_V).astype(d_cq.dtype)

def depthwise_conv(u, w, bias):
    c = u.shape[-1]
    y = lax.conv_general_dilated(u, w[:, None, :].astype(u.dtype), window_strides=(1,), padding='SAME',
                                 dimension_numbers=('NWC', 'WIO', 'NWC'), feature_group_count=c)
    return y + bias.astype(u.dtype)

def hybrid_layer(x, pos, layer_idx, norm1_g, w_in, a_q_norm, a_k_norm, a_sink, b_q_norm, b_k_norm,
                 b_lam_q1, b_lam_k1, b_lam_q2, b_lam_k2, b_subln_g, c_q_norm, c_k_norm, d_cq_norm,
                 d_ckv_norm, d_w_uq, d_w_ukv, d_q_norm, d_k_norm, w_branch, w_o, norm2_g, ffn_w_up,
                 ffn_conv_w, ffn_conv_b, ffn_w_down):
    h = rms_norm(x, norm1_g)
    (a_q, a_k, a_v, b_q, b_k, b_v, c_qkv, d_cq, d_ckv, d_kr, gates) = jnp.split(
        h @ w_in, _split_points(IN_SPLITS), axis=-1)
    lam_init = 0.8 - 0.6 * math.exp(-0.3 * layer_idx)
    oa = windowed_gqa(a_q, a_k, a_v, pos, a_q_norm, a_k_norm, a_sink)
    ob = differential_attention(b_q, b_k, b_v, pos, b_q_norm, b_k_norm, b_lam_q1, b_lam_k1,
                                b_lam_q2, b_lam_k2, b_subln_g, lam_init)
    oc = dilated_attention(c_qkv, pos, c_q_norm, c_k_norm)
    od = latent_attention(d_cq, d_ckv, d_kr, pos, d_cq_norm, d_ckv_norm, d_w_uq, d_w_ukv, d_q_norm, d_k_norm)
    merged = jnp.zeros_like(x)
    for i, o in enumerate((oa, ob, oc, od)):
        gate = jax.nn.sigmoid(gates[..., i * D_MODEL:(i + 1) * D_MODEL])
        merged = merged + gate * (o @ w_branch[i])
    x = x + merged @ w_o
    u = depthwise_conv(rms_norm(x, norm2_g) @ ffn_w_up, ffn_conv_w, ffn_conv_b)
    g, up = jnp.split(u, 2, axis=-1)
    return x + (jax.nn.silu(g) * up) @ ffn_w_down

def setup_inputs(seed: int = 0) -> dict:
    key = jax.random.key(seed)
    ks = iter(jax.random.split(key, 40))
    f32 = jnp.float32
    L = DEPTH

    def nrm(shape, scale):
        return jax.random.normal(next(ks), shape, f32) * scale

    def gain(shape):
        return 1.0 + nrm(shape, 0.05)

    x = jax.random.normal(next(ks), (BATCH, SEQ, D_MODEL), f32)
    positions = (jnp.arange(SEQ, dtype=jnp.int32)[None, :]
                 + jax.random.randint(next(ks), (BATCH, 1), 0, 4096, dtype=jnp.int32))
    return {
        "x": x,
        "positions": positions,
        "norm1_g": gain((L, D_MODEL)),
        "w_in": nrm((L, D_MODEL, N_IN), D_MODEL ** -0.5),
        "a_q_norm": gain((L, HEAD_DIM)),
        "a_k_norm": gain((L, HEAD_DIM)),
        "a_sink": nrm((L, A_Q_HEADS), 0.5),
        "b_q_norm": gain((L, HEAD_DIM)),
        "b_k_norm": gain((L, HEAD_DIM)),
        "b_lam_q1": nrm((L, B_HEADS, HEAD_DIM), 0.1),
        "b_lam_k1": nrm((L, B_HEADS, HEAD_DIM), 0.1),
        "b_lam_q2": nrm((L, B_HEADS, HEAD_DIM), 0.1),
        "b_lam_k2": nrm((L, B_HEADS, HEAD_DIM), 0.1),
        "b_subln_g": gain((L, B_V_DIM)),
        "c_q_norm": gain((L, HEAD_DIM)),
        "c_k_norm": gain((L, HEAD_DIM)),
        "d_cq_norm": gain((L, D_Q_RANK)),
        "d_ckv_norm": gain((L, D_KV_RANK)),
        "d_w_uq": nrm((L, D_Q_RANK, D_HEADS * (D_NOPE + D_ROPE)), D_Q_RANK ** -0.5),
        "d_w_ukv": nrm((L, D_KV_RANK, D_HEADS * (D_NOPE + D_V)), D_KV_RANK ** -0.5),
        "d_q_norm": gain((L, D_NOPE + D_ROPE)),
        "d_k_norm": gain((L, D_NOPE + D_ROPE)),
        "w_branch": nrm((L, N_BRANCH, BRANCH_WIDTH, D_MODEL), BRANCH_WIDTH ** -0.5),
        "w_o": nrm((L, D_MODEL, D_MODEL), D_MODEL ** -0.5),
        "norm2_g": gain((L, D_MODEL)),
        "ffn_w_up": nrm((L, D_MODEL, 2 * D_FF), D_MODEL ** -0.5),
        "ffn_conv_w": nrm((L, CONV_WIDTH, 2 * D_FF), CONV_WIDTH ** -0.5),
        "ffn_conv_b": nrm((L, 2 * D_FF), 0.01),
        "ffn_w_down": nrm((L, D_FF, D_MODEL), D_FF ** -0.5),
    }

def reference(x, positions, norm1_g, w_in, a_q_norm, a_k_norm, a_sink, b_q_norm, b_k_norm,
              b_lam_q1, b_lam_k1, b_lam_q2, b_lam_k2, b_subln_g, c_q_norm, c_k_norm, d_cq_norm,
              d_ckv_norm, d_w_uq, d_w_ukv, d_q_norm, d_k_norm, w_branch, w_o, norm2_g, ffn_w_up,
              ffn_conv_w, ffn_conv_b, ffn_w_down):
    for l in range(DEPTH):
        x = hybrid_layer(x, positions, l, norm1_g[l], w_in[l], a_q_norm[l], a_k_norm[l], a_sink[l],
                         b_q_norm[l], b_k_norm[l], b_lam_q1[l], b_lam_k1[l], b_lam_q2[l], b_lam_k2[l],
                         b_subln_g[l], c_q_norm[l], c_k_norm[l], d_cq_norm[l], d_ckv_norm[l], d_w_uq[l],
                         d_w_ukv[l], d_q_norm[l], d_k_norm[l], w_branch[l], w_o[l], norm2_g[l],
                         ffn_w_up[l], ffn_conv_w[l], ffn_conv_b[l], ffn_w_down[l])
    return x


_drawn_inputs = setup_inputs


def setup_inputs(seed=0):
    import zlib

    import numpy as np

    out = dict(_drawn_inputs(seed))
    spreads = {}
    factors = {'a_q_norm': 7.418,
     'a_k_norm': 6.591,
     'a_sink': 8.0,
     'c_q_norm': 6.926,
     'c_k_norm': 6.854,
     'd_cq_norm': 8.0,
     'd_ckv_norm': 8.0,
     'd_q_norm': 8.0,
     'd_k_norm': 8.0,
     'ffn_conv_b': 5.657}
    for name, (base, spread) in spreads.items():
        noise = np.random.default_rng([zlib.crc32(name.encode()), seed]).standard_normal(out[name].shape)
        drawn = base * np.exp(spread * noise) if base else spread * noise
        out[name] = jnp.asarray(drawn.astype(out[name].dtype))
    for name, factor in factors.items():
        out[name] = (out[name] * factor).astype(out[name].dtype)
    return out
```

```python
import math
from contextlib import ExitStack

import numpy as np
import concourse.bass as bass
from concourse import mybir

F32 = mybir.dt.float32
F32R = mybir.dt.float32r
I32 = mybir.dt.int32
ALU = mybir.AluOpType
ACT = mybir.ActivationFunctionType
AXX = mybir.AxisListType.X

P = 128
DM, SEQ, DEPTH = 1024, 512, 2
TT = SEQ // P
DC = DM // P
HD = 64
FF = 2816
BW = 512
A_RADIUS = 128
C_PATTERNS = ((128, 1), (512, 4), (2048, 16))
RES = 4
QR, KVR, NOPE, ROPE, DV = 384, 256, 64, 32, 64
DQK = NOPE + ROPE
EPS = 1e-6
MASKED = 1e30
SCALE = HD ** -0.5
COL = dict(Aq=0, Akv=512, B=768, C=2304, cq=6912, ckv=7296, kr=7552, gate=7584)
LAT_Q, LAT_KV = 4, 7
HALF = 384 * 3
UP_GROUPS = (4, 4, 3)

ROW = dict(norm1=0, norm2=8, cq=16, ckv=19, subln=21, aq=22, ak=23, bq=24, bk=25, cqn=26, ckn=27, dq=28, dk=29)
NROW = 30
CONV_B = FF * 2 // P
PRM_CONV = NROW

A_SLOPES = [2.0 ** (-8.0 * (i + 1) / 8) for i in range(8)]
B_SLOPES = [2.0 ** (-8.0 * (i + 1) / 4) for i in range(4)]
C_SLOPES = [[2.0 ** (-8.0 * (j * 8 + i + 1) / 24) for i in range(8)] for j in range(3)]


def shape_constants():
    i = np.arange(P)[:, None, None]
    t = np.arange(TT)[None, :, None]
    j = np.arange(SEQ)[None, None, :]
    mask_a = np.where(np.abs(P * t + i - j) <= A_RADIUS, 0.0, MASKED)
    mask_c0 = np.where(np.abs(RES * i + t - j) <= C_PATTERNS[0][0] // 2, 0.0, MASKED)
    q, k = np.arange(P)[:, None], np.arange(P)[None, :]
    mask_c1 = np.where(np.abs(q - k) <= C_PATTERNS[1][0] // 8, 0.0, MASKED)
    mask_c2 = np.where((q - k) % 4 == 0, 0.0, MASKED)
    consts = np.zeros((P, 128 + 20 + 16), np.float32)
    consts[:, :P] = np.eye(P)
    for c in range(4):
        for half in range(2):
            rows = slice(64 * half, 64 * half + 64)
            h = 2 * c + half
            consts[rows, 128 + c] = -SCALE / A_SLOPES[h]
            consts[rows, 132 + c] = -SCALE / B_SLOPES[h % 4]
            for n in range(3):
                consts[rows, 136 + 4 * n + c] = -SCALE / C_SLOPES[n][h]
    consts[:, 148:164] = 10000.0 ** (-np.arange(16, dtype=np.float32) / np.float32(16))
    lam = np.array([[0.8 - 0.6 * math.exp(-0.3 * n), 0.2 + 0.6 * math.exp(-0.3 * n)] for n in range(DEPTH)])
    return dict(
        k_mask_a=mask_a.astype(np.float32), k_mask_c0=mask_c0.astype(np.float32),
        k_mask_c12=np.stack([mask_c1, mask_c2], 1).astype(np.float32),
        k_consts=consts, k_lam=lam.astype(np.float32),
    )


class Signal:

    def __init__(self, handle, before, each, unit=1):
        self.handle, self.before, self.each, self.unit, self.n = handle, before, each, unit, 0

    def at(self, layer, k):
        return self.handle, self.unit * (layer * self.each + self.before + k)

    def up(self, own=None):
        self.n += 1
        if own is not None:
            own.last, own.k = self, self.n
        return self.handle, self.unit


class Own:

    def __init__(self, last, k=0):
        self.last, self.k = last, k

    def done(self, layer):
        return self.last.at(layer, self.k)


EACH = dict(
    raw_landed0=119, raw_landed1=119, hi_split=186, tile_split=186, tile_used=132, pj_ready=216, pj_act=108,
    pj_dve=108, sq_ready=60, sq_used=60, normed=78, tp_ready=237, tp_act=237, tp_dve=237, s_ready=144,
    s_biased=144, p_ready=144, o_ready=144, o_out=144, gains_in=1, ssum=16, lam_dot=1, lam_exp=1, c_diff=1,
    c_exp=1, merged_sum=24, merged_hi=8, merged_lo=8, conv_mid=44, e_ready=22, hidden_val=22, hidden_hi=22,
    hidden_lo=22, act_step=129, dve_step=531, params_in=22, direct_in=8, x_moved=2,
)


def build(nc, io):
    ctx = ExitStack()
    with ctx:
        _build(nc, io, ctx)


def _build(nc, io, ctx):
    def sb(name, shape, dt=F32):
        return ctx.enter_context(nc.sbuf_tensor("s_" + name, shape, dt))

    signals, wrong = {}, {}

    def signal(name, before=0, unit=1):
        s = Signal(ctx.enter_context(nc.semaphore(name)), before, EACH.get(name, 0), unit)
        signals[name] = s
        return s

    def sem(name):
        return ctx.enter_context(nc.semaphore(name))

    hTh, hTl = sb("hTh", [P, DC, SEQ], F32R), sb("hTl", [P, DC, SEQ], F32R)
    gTh, gTl = sb("gTh", [P, DC + 1, SEQ], F32R), sb("gTl", [P, DC + 1, SEQ], F32R)
    raw = sb("raw", [P, 2, HALF])
    wh, wl = sb("wh", [P, 2, HALF], F32R), sb("wl", [P, 2, HALF], F32R)
    bias = sb("bias", [P, 14, SEQ])
    work = sb("work", [P, 19968])
    consts = sb("consts", [P, 164])
    rows = sb("rows", [P, 3, P])
    prm = sb("prm", [P, NROW + 4 * CONV_B])
    gain = sb("gain", [P, 24])
    rope_rows = sb("rope_rows", [P, 2, ROPE])
    trig = sb("trig", [P, 2, TT, 16])
    sink = sb("sink", [P, 8])
    one = sb("one", [P, 1])
    lamc = sb("lamc", [P, 2])
    lam = sb("lam", [P, 8])
    stat = sb("stat", [P, 16, 32])
    krr = sb("krr", [P, TT, ROPE])

    ident = consts[:, 0:P]
    bias_a, bias_b, bias_c0 = bias[:, 0:4, :], bias[:, 4:8, :], bias[:, 8:12, :]
    bias_c12 = bias[:, 12:14, :]
    stage = work[:, 0:2048].rearrange("p (t n) -> p t n", t=4)
    sq = work[:, 2048:3072].rearrange("p (s n) -> p s n", s=2)
    kdup = work[:, 3072:4096].rearrange("p (t n) -> p t n", t=4)
    scores = work[:, 0:1024].rearrange("p (s n) -> p s n", s=2)
    probs = work[:, 1024:2048].rearrange("p (s n) -> p s n", s=2)
    probsT = work[:, 2048:3072].rearrange("p (s n) -> p s n", s=2)
    otok = work[:, 3072:4096].rearrange("p (s n) -> p s n", s=2)
    AD = 4096
    qT = work[:, AD:AD + 2048].rearrange("p (c n) -> p c n", c=4)
    kT = work[:, AD + 2048:AD + 4096].rearrange("p (c n) -> p c n", c=4)
    vB = work[:, AD + 4096:AD + 6144].rearrange("p (t n) -> p t n", t=4)
    oC = work[:, AD + 6144:AD + 12288].rearrange("p (j t n) -> p j t n", j=3, t=4)
    qD = work[:, AD:AD + 4096].rearrange("p (h n) -> p h n", h=8)
    kD = work[:, AD + 4096:AD + 8192].rearrange("p (h n) -> p h n", h=8)
    vD = work[:, AD + 8192:AD + 10240].rearrange("p (t n) -> p t n", t=4)
    kA = work[:, AD + 10240:AD + 11264].rearrange("p (g n) -> p g n", g=2)
    vA = work[:, AD + 11264:AD + 11776].rearrange("p (t n) -> p t n", t=4)
    merged = work[:, AD + 11776:AD + 15872].rearrange("p (c n) -> p c n", c=8)
    x_sb = work[:, AD:AD + 4096].rearrange("p (t n) -> p t n", t=4)
    h_sb = work[:, AD + 4096:AD + 8192].rearrange("p (t n) -> p t n", t=4)
    hid = work[:, AD + 4096:AD + 6144].rearrange("p (m n) -> p m n", m=4)
    act_e = work[:, AD + 6144:AD + 7168].rearrange("p (m n) -> p m n", m=2)
    lam_in = work[:, AD + 8192:AD + 9216].rearrange("p (v n) -> p v n", v=4)
    gates = work[:, AD + 6144:AD + 8192].rearrange("p (t n) -> p t n", t=4)
    oB = gates
    trig_angle, trig_abs = work[:, 1600:1664], work[:, 1664:1728]
    rope_tmp = work[:, 3072:3584]
    branch_tmp = work[:, 2048:3072].rearrange("p (s n) -> p s n", s=2)

    bank = [ctx.enter_context(nc.psum_tensor(f"bank{i}", [P, 512], F32)) for i in range(8)]
    PJ = bank[0:4]
    SB = bank[4:6]
    OB = bank[2:4]
    TP = bank[6:8]

    x_keep = nc.dram_tensor("x_keep", (SEQ, DM), F32).ap()

    raw_landed = [signal("raw_landed0", unit=16), signal("raw_landed1", unit=16)]
    hi_split = signal("hi_split")
    tile_split = signal("tile_split", before=2)
    tile_used = signal("tile_used", before=1)
    pj_ready = signal("pj_ready", before=1)
    pj_act = signal("pj_act")
    pj_dve = signal("pj_dve", before=8)
    sq_ready = signal("sq_ready")
    sq_used = signal("sq_used")
    normed = signal("normed")
    tp_ready = signal("tp_ready")
    tp_act = signal("tp_act", before=2)
    tp_dve = signal("tp_dve", before=2)
    s_ready = signal("s_ready")
    s_biased = signal("s_biased", before=1)
    p_ready = signal("p_ready")
    o_ready = signal("o_ready")
    o_out = signal("o_out")
    gains_in = signal("gains_in")
    ssum = signal("ssum")
    lam_dot = signal("lam_dot")
    lam_exp = signal("lam_exp")
    c_diff = signal("c_diff")
    c_exp = signal("c_exp")
    merged_sum = signal("merged_sum")
    merged_hi = signal("merged_hi")
    merged_lo = signal("merged_lo")
    conv_mid = signal("conv_mid")
    e_ready = signal("e_ready")
    hidden_val = signal("hidden_val")
    hidden_hi = signal("hidden_hi")
    hidden_lo = signal("hidden_lo")
    act_step = signal("act_step", before=1)
    dve_step = signal("dve_step", before=1)
    params_in = signal("params_in", before=22, unit=16)
    direct_in = signal("direct_in", unit=16)
    x_moved = signal("x_moved", unit=16)
    setup_in = sem("setup_in")
    setup_act = sem("setup_act")
    setup_dve = sem("setup_dve")
    dve_setup = sem("dve_setup")
    x_in = sem("x_in")
    out_done = sem("out_done")
    waits_met = sem("waits_met")
    rows_clear = sem("rows_clear")

    nc.disable_value_cache = True

    def layers(eng):
        return eng.Fori(0, DEPTH)

    def weight_tiles(l):
        def chunk_rows(w, kt, chunks=2):
            return w[bass.ds(l, 1), kt * P * chunks:(kt + 1) * P * chunks, :].rearrange("a (c p) n -> p (a c) n", p=P)

        w_in, w_up, w_down = io["w_in"], io["ffn_w_up"], io["ffn_w_down"]
        w_br = io["w_branch"].rearrange("l b k n -> l (b k) n")

        def block(w, *cols, kts=range(4)):
            for kt in kts:
                at, pieces = 0, []
                for c0, n in cols:
                    pieces.append((at, n, chunk_rows(w, kt)[:, :, c0:c0 + n]))
                    at += n
                yield pieces, 2, at, kt == kts[-1]

        def gate(i, cb):
            yield from block(w_in, (COL["gate"] + i * DM + cb * BW, BW))

        def branch(i, cb):
            yield from block(w_br, (cb * BW, BW), kts=range(2 * i, 2 * i + 2))

        def gate_and_branch(i):
            for cb in range(2):
                yield from gate(i, cb)
                yield from branch(i, cb)

        def d_up(w, hb):
            if w == "q":
                yield [(0, QR, chunk_rows(io["d_w_uq"], 0, 3)[:, :, hb * 384:hb * 384 + 384])], 3, 384, True
            else:
                yield from block(io["d_w_ukv"], (hb * BW, BW), kts=range(1))

        for b in range(9):
            yield from block(w_in, (COL["C"] + b * BW, BW))
        yield from block(w_in, (COL["Akv"], 256), (COL["ckv"], KVR))
        yield from block(w_in, (COL["cq"], QR), (COL["kr"], ROPE))
        yield from gate(2, 0)
        yield from d_up("q", 0)
        yield from branch(2, 0)
        yield from d_up("q", 1)
        yield from gate(2, 1)
        yield from d_up("kv", 0)
        yield from branch(2, 1)
        yield from d_up("kv", 1)
        yield from block(w_in, (COL["Aq"], BW))
        yield from gate_and_branch(3)
        for b in range(3):
            yield from block(w_in, (COL["B"] + b * BW, BW))
        yield from gate_and_branch(0)
        yield from gate_and_branch(1)
        for cb in range(2):
            yield from block(io["w_o"], (cb * BW, BW))
        first = 0
        for n in UP_GROUPS:
            for b in range(first, first + n):
                yield from block(w_up, (256 * b, 256), (FF + 256 * b, 256))
            for cb in range(2):
                yield from block(w_down, (cb * BW, BW), kts=range(first, first + n))
            first += n

    def all_keys(u):
        return 0, TT, TT // 2

    def near_keys(u):
        t = u // 8
        reach = -(-A_RADIUS // P)
        lo, hi = max(0, t - reach), min(TT, t + reach + 1)
        return lo, hi, (lo + hi + 1) // 2

    def parameter_rows(layer):
        at = bass.ds(layer, 1)
        for name, key in (("norm1_g", "norm1"), ("norm2_g", "norm2"), ("d_cq_norm", "cq"), ("d_ckv_norm", "ckv"),
                          ("b_subln_g", "subln")):
            src = io[name][at].rearrange("a (r c) -> (a r) c", c=P)
            yield rows[ROW[key]:ROW[key] + src.shape[0], 0, :], src
        for name, key in (("a_q_norm", "aq"), ("a_k_norm", "ak"), ("b_q_norm", "bq"), ("b_k_norm", "bk"),
                          ("c_q_norm", "cqn"), ("c_k_norm", "ckn")):
            for half in range(2):
                yield rows[ROW[key]:ROW[key] + 1, 0, HD * half:HD * half + HD], io[name][at, :]
        yield rows[ROW["dq"]:ROW["dq"] + 1, 0, 0:NOPE], io["d_q_norm"][at, 0:NOPE]
        yield rows[ROW["dk"]:ROW["dk"] + 1, 0, 0:NOPE], io["d_k_norm"][at, 0:NOPE]
        conv_w = io["ffn_conv_w"][at].rearrange("a k (r c) -> (a k r) c", c=P)
        yield rows[0:88, 1, :], conv_w[0:88, :]
        yield rows[0:44, 2, :], conv_w[88:132, :]
        yield rows[44:88, 2, :], io["ffn_conv_b"][at].rearrange("a (r c) -> (a r) c", c=P)

    def norm_bank(g0, c):
        return (TP[g0 % 2], TP[(g0 + 1) % 2], SB[0], SB[1])[c % 4]

    block_ = ctx.enter_context(nc.Block())

    @block_.sync
    def _(sp):
        for dst, src in ((consts[:], io["k_consts"]), (bias_a, io["k_mask_a"]), (bias_c0, io["k_mask_c0"]),
                         (work[:, 0:256].rearrange("p (m n) -> p m n", m=2), io["k_mask_c12"]),
                         (work[:, 512:1024].bitcast(I32), io["positions"][0, :].partition_broadcast(P)),
                         (work[:, 256:260].bitcast(I32), io["positions"].rearrange("a (t p) -> p (a t)", p=P)),
                         (work[:, 260:264].bitcast(I32), io["positions"].rearrange("a (p r) -> p (a r)", r=RES))):
            sp.dma_start(dst, src, allow_slow_non_contiguous=True).then_inc(setup_in, 16)
        sp.dma_start(x_sb, io["x"].rearrange("a (t p) n -> p (a t) n", p=P)).then_inc(x_in, 16)
        with layers(sp) as l:
            for k, (pieces, chunks, cols, _last) in enumerate(weight_tiles(l)):
                sp.wait_ge(*tile_split.at(l, k - 1))
                dst = raw[:, k % 2, 0:chunks * cols].rearrange("p (c n) -> p c n", c=chunks)
                for at, n, src in pieces:
                    sp.dma_start(dst[:, :, at:at + n], src).then_inc(*(raw_landed[k % 2]).up())
        sp.wait_ge(*pj_dve.at(DEPTH, 0))
        sp.dma_start(io["y"].rearrange("a (t p) n -> p (a t) n", p=P), x_sb).then_inc(out_done, 16)
        sp.wait_ge(out_done, 16)

    @block_.gpsimd
    def _(pool):
        for s in (tile_split, tile_used, pj_ready, pj_dve, tp_act, tp_dve, s_biased, act_step, dve_step):
            pool.sem_inc(s.handle, s.before)
        pool.memset(rows[:], 1.0).then_inc(rows_clear, 1)
        pool.memset(one[:], 1.0).then_inc(rows_clear, 1)
        pool.wait_ge(rows_clear, 2)
        with layers(pool) as l:
            landed = [0, 0]
            released = [(tile_used, 0), (pj_ready, 0)]
            used = ready = 0
            for k, (pieces, chunks, cols, last) in enumerate(weight_tiles(l)):
                s, n = k % 2, chunks * cols
                landed[s] += len(pieces)
                pool.wait_ge(*raw_landed[s].at(l, landed[s]))
                user, count = released[k]
                pool.wait_ge(*user.at(l, count))
                src = raw[:, s, 0:n]
                pool.tensor_tensor(wh[:, s, 0:n], src, one[:].to_broadcast([P, n]), ALU.mult).then_inc(*hi_split.up())
                pool.wait_ge(*hi_split.at(l, hi_split.n))
                pool.tensor_tensor(wl[:, s, 0:n], src, wh[:, s, 0:n].bitcast(F32), ALU.subtract).then_inc(*tile_split.up())
                if last:
                    ready += 4
                else:
                    used += 1
                released.append((pj_ready, ready) if last else (tile_used, used))

    @block_.tensor
    def _(pe):
        mm = nc.tensor.matmul
        pe.wait_ge(setup_in, 16 * 7)

        with layers(pe) as l:
            n_tile, n_group, n_unit, n_normed = [0], [0], [0], [0]
            taken = {pj_act: 0, pj_dve: 0}
            holder = [(pj_dve, b - 3) for b in range(4)]

            def split3(out, stationary, moving, start, stop):
                mm(out, stationary[0], moving[0], start=start, stop=False)
                mm(out, stationary[0], moving[1], start=False, stop=False)
                return mm(out, stationary[1], moving[0], start=False, stop=stop)

            def block(ntiles, operands, by, chunks=2, cols=512, width=512, hooks=(), before=None):
                step = 0
                for i in range(ntiles):
                    s = n_tile[0] % 2
                    pe.wait_ge(*tile_split.at(l, n_tile[0] + 1))
                    w = [t[:, s, 0:chunks * cols].rearrange("p (c n) -> p c n", c=chunks) for t in (wh, wl)]
                    for b in range(4):
                        if i == 0:
                            taker, count = holder[b]
                            pe.wait_ge(*taker.at(l, count))
                            taken[by] += 1
                            holder[b] = (by, taken[by])
                        if before is not None:
                            before(i, b)
                        for c in range(chunks):
                            st, mv = operands(b, chunks * i + c, [t[:, c, :] for t in w])
                            last = split3(PJ[b][:, 0:width], st, mv, i == 0 and c == 0, i == ntiles - 1 and c == chunks - 1)
                        if i == ntiles - 1:
                            last.then_inc(*pj_ready.up())
                        elif b == 3:
                            last.then_inc(*tile_used.up())
                        step += 1
                        for after, between in hooks:
                            if after == step:
                                between()
                    n_tile[0] += 1

            def tokens_out(act, first=0, perm=False):
                def operands(b, kc, w):
                    views = [a[:, first + kc, :] for a in act]
                    if perm:
                        views = [v.rearrange("p (i r) -> p r i", r=RES)[:, b, :] for v in views]
                    else:
                        views = [v[:, P * b:P * b + P] for v in views]
                    return views, w
                return operands

            def features_out(act, first=0):
                def operands(b, kc, w):
                    return [t[:, P * b:P * b + P] for t in w], [a[:, first + kc, :] for a in act]
                return operands

            H, G = (hTh, hTl), (gTh, gTl)

            def transposes(sources, at=0):
                g = n_group[0]
                pe.wait_ge(*tp_act.at(l, g - 1))
                pe.wait_ge(*tp_dve.at(l, g - 1))
                for n, src in enumerate(sources, at):
                    k, m = src.shape[0], src.shape[1]
                    last = nc.tensor.transpose(TP[g % 2][0:m, n * P:n * P + k], src, ident[0:k, 0:k])
                n_group[0] += 1
                last.then_inc(*tp_ready.up())

            def norm_transposes():
                n_normed[0] += 4
                pe.wait_ge(*normed.at(l, n_normed[0]))
                g0 = n_group[0]
                for c in range(DC):
                    g = n_group[0]
                    if c < 2:
                        pe.wait_ge(*tp_act.at(l, g - 1))
                        pe.wait_ge(*tp_dve.at(l, g - 1))
                    elif c < 4:
                        pe.wait_ge(*s_biased.at(l, n_unit[0]))
                    else:
                        pe.wait_ge(*tp_act.at(l, g - 3))
                        pe.wait_ge(*tp_dve.at(l, g - 3))
                    dst = norm_bank(g0, c)
                    for t in range(4):
                        last = nc.tensor.transpose(dst[:, t * P:t * P + P], h_sb[:, t, P * c:P * c + P], ident)
                    n_group[0] += 1
                    last.then_inc(*tp_ready.up())

                def chunks_out(i, b):
                    if b == 0:
                        pe.wait_ge(*tp_act.at(l, g0 + 2 * i + 2))
                        pe.wait_ge(*tp_dve.at(l, g0 + 2 * i + 2))
                return chunks_out

            def normed_transposes(sources):
                n_normed[0] += 1
                pe.wait_ge(*normed.at(l, n_normed[0]))
                transposes(sources)

            def transposed_out():
                pe.wait_ge(*tp_act.at(l, n_group[0]))
                pe.wait_ge(*tp_dve.at(l, n_group[0]))

            def hook_groups(make, at=(7, 9, 11, 13)):
                return [(at[t], lambda t=t: normed_transposes(make(t))) for t in range(4)]

            def score(u, scores_of):
                for out, st, mv in scores_of(u, SB[u % 2]):
                    last = mm(out, st, mv, start=True, stop=True)
                last.then_inc(*s_ready.up())

            def first_scores(scores_of, at):
                def start(u):
                    transposed_out()
                    score(u, scores_of)
                return [(at, lambda: start(0)), (at + 1, lambda: start(1))]

            def attention(n, scores_of, values_of, keys=all_keys, started=0, tile_out=None):
                if not started:
                    transposed_out()
                    pe.wait_ge(*pj_act.at(l, taken[pj_act]))
                first, group = n_unit[0], {}
                for step in range(started, n + 3):
                    if step < n:
                        if step >= 2:
                            pe.wait_ge(*s_biased.at(l, first + step - 1))
                        score(step, scores_of)
                    if 2 <= step < n + 2:
                        u = step - 2
                        pe.wait_ge(*p_ready.at(l, first + u + 1))
                        group[u] = n_group[0]
                        lo, hi, _mid = keys(u)
                        transposes([probs[:, u % 2, P * k:P * k + P] for k in range(lo, hi)], at=lo)
                    if step >= 3:
                        u = step - 3
                        pe.wait_ge(*tp_act.at(l, group[u] + 1))
                        pe.wait_ge(*tp_dve.at(l, group[u] + 1))
                        if u >= 2:
                            pe.wait_ge(*o_out.at(l, first + u - 1))
                        elif started and u == 0:
                            pe.wait_ge(*pj_act.at(l, taken[pj_act]))
                            pe.wait_ge(*pj_dve.at(l, taken[pj_dve]))
                        for out, st, mv, start, stop in values_of(u, OB[u % 2], probsT[:, u % 2, :]):
                            last = mm(out, st, mv, start=start, stop=stop)
                        last.then_inc(*o_ready.up())
                    if tile_out and step >= 12 and (step - 12) % 8 == 0:
                        tile_out((step - 12) // 8)
                n_unit[0] += n
                holder[2] = holder[3] = (o_out, n_unit[0])

            def dense_values(v_of, width, keys=all_keys):
                def values_of(u, out, pt):
                    lo, hi, _mid = keys(u)
                    return [(out[:, 0:width], pt[:, P * k:P * k + P], v_of(u, k), k == lo, k == hi - 1) for k in range(lo, hi)]
                return values_of

            def gate_block(hooks=()):
                block(4, features_out(H), pj_act, hooks=hooks)

            def branch_block(hooks=()):
                transposed_out()
                block(2, features_out(G), pj_dve, hooks=hooks)

            def gates_and_branch(hooks=(), last_hooks=()):
                for cb in range(2):
                    gate_block(hooks if cb == 0 else ())
                    branch_block(last_hooks if cb == 1 else ())

            def q_tile(h, t):
                return qT[64 * (h % 2):64 * (h % 2) + 64, h // 2, P * t:P * t + P]

            def out_tiles(t):
                return [otok[:, t % 2, P * c:P * c + P] for c in range(4)]

            pe.wait_ge(*params_in.at(l, 0))
            transposes([rows[:, n, :] for n in range(3)])
            chunks_out = norm_transposes()

            staged = lambda t: [stage[:, t, P * c:P * c + P] for c in range(4)]
            for j in range(3):
                if j == 0:
                    scores_of = lambda u, out: [(out[:], q_tile(u % 8, u // 8),
                                                 kT[64 * (u % 2):64 * (u % 2) + 64, (u % 8) // 2, :])]
                    values_of = dense_values(lambda u, k: vB[:, k, HD * (u % 8):HD * (u % 8) + HD], HD)
                else:
                    scores_of = lambda h, out: [(out[:, P * r:P * r + P], q_tile(h, r),
                                                 kT[64 * (h % 2):64 * (h % 2) + 64, h // 2, P * r:P * r + P])
                                                for r in range(RES)]
                    values_of = lambda h, out, pt: [(out[:, HD * r:HD * r + HD], pt[:, P * r:P * r + P],
                                                     vB[:, r, HD * h:HD * h + HD], True, True) for r in range(RES)]
                block(4, tokens_out(H, perm=True), pj_act, before=chunks_out if j == 0 else None)
                block(4, tokens_out(H, perm=j > 0), pj_act, hooks=hook_groups(staged))
                block(4, tokens_out(H, perm=j > 0), pj_act,
                      hooks=hook_groups(staged, at=(7, 9, 10, 12)) + first_scores(scores_of, 14))
                attention(8 if j else 32, scores_of, values_of, started=2)

            block(4, tokens_out(H), pj_act, hooks=hook_groups(lambda t: [oC[:, 0, t, P * c:P * c + P] for c in range(4)], at=(9, 10, 11, 12)))
            block(4, tokens_out(H), pj_act, cols=416, width=416, hooks=hook_groups(
                lambda t: [kdup[:, t, 0:P], kdup[:, t, P:2 * P], stage[:, t, 256:384], stage[:, t, 384:512]], at=(12, 13, 14, 15)))
            gate_block(hook_groups(lambda t: [stage[:, t, P * c:P * c + P] for c in range(3)], at=(10, 11, 12, 13)))
            dq_tiles = lambda t: [stage[:, t, DQK * h:DQK * h + DQK] for h in range(4)]
            dk_tiles = lambda t: [stage[:, t, P * h:P * h + DQK] for h in range(4)]
            transposed_out()
            block(1, tokens_out(G, first=LAT_Q), pj_act, chunks=3, cols=384, width=384)
            branch_block()
            n_normed[0] += 1
            pe.wait_ge(*normed.at(l, n_normed[0]))
            for t in range(4):
                transposes(dq_tiles(t))
            block(1, tokens_out(G, first=LAT_Q), pj_act, chunks=3, cols=384, width=384)
            gate_block([(10, lambda: normed_transposes(dq_tiles(0)))] + [(10 + t, lambda t=t: transposes(dq_tiles(t))) for t in (1, 2, 3)])
            block(1, tokens_out(G, first=LAT_KV), pj_act)
            branch_block()
            for t in range(4):
                normed_transposes(dk_tiles(t))
            block(1, tokens_out(G, first=LAT_KV), pj_act)
            for t in range(4):
                normed_transposes(dk_tiles(t))
            attention(32, lambda u, out: [(out[:], qD[0:DQK, u % 8, P * (u // 8):P * (u // 8) + P], kD[0:DQK, u % 8, :])],
                      dense_values(lambda u, k: vD[:, k, DV * (u % 8):DV * (u % 8) + DV], DV),
                      tile_out=lambda t: normed_transposes(out_tiles(t)))

            last_tile = [(2, lambda: normed_transposes(out_tiles(3)))]
            block(4, tokens_out(H), pj_act, hooks=last_tile)

            def a_scores(u, out):
                lo, hi, _mid = near_keys(u)
                return [(out[:, P * lo:P * hi], q_tile(u % 8, u // 8),
                         kA[64 * (u % 2):64 * (u % 2) + 64, (u % 8) // 4, P * lo:P * hi])]
            gates_and_branch(hook_groups(staged), first_scores(a_scores, 3))
            attention(32, a_scores,
                      dense_values(lambda u, k: vA[:, k, HD * ((u % 8) // 4):HD * ((u % 8) // 4) + HD], HD, near_keys),
                      keys=near_keys, started=2, tile_out=lambda t: normed_transposes(out_tiles(t)))

            block(4, tokens_out(H), pj_act, hooks=last_tile)
            block(4, tokens_out(H), pj_act, hooks=hook_groups(staged))
            block(4, tokens_out(H), pj_act, hooks=hook_groups(staged))

            def b_scores(u, out):
                t, h, m = u // 8, (u % 8) // 2, u % 2
                n = 4 * m + h
                return [(out[:], q_tile(n, t), kT[64 * (n % 2):64 * (n % 2) + 64, n // 2, :])]
            gates_and_branch((), first_scores(b_scores, 3))
            attention(32, b_scores, dense_values(lambda u, k: vB[:, k, P * ((u % 8) // 2):P * ((u % 8) // 2) + P], P),
                      started=2)
            gates_and_branch(hook_groups(lambda t: [oB[:, t, P * c:P * c + P] for c in range(4)], at=(9, 10, 11, 12)))

            for cb in range(2):
                block(4, tokens_out(H), pj_dve,
                      before=lambda i, b: pe.wait_ge(*merged_lo.at(l, 2 * i + 2)) if cb == 0 and b == 0 else None)
            chunks_out = norm_transposes()
            hidden = 0
            for group in UP_GROUPS:
                for b in range(group):
                    block(4, features_out(H), pj_dve, before=chunks_out if hidden == 0 and b == 0 else None)
                for cb in range(2):
                    block(group, tokens_out(G), pj_dve,
                          before=lambda i, b: pe.wait_ge(*hidden_lo.at(l, hidden + 2 * i + 2)) if cb == 0 and b == 0 else None)
                hidden += 2 * group

    @block_.scalar
    def _(act):
        a = nc.scalar.activation
        act.wait_ge(rows_clear, 1)
        for dst, src in parameter_rows(0):
            act.dma_start(dst, src, allow_slow_non_contiguous=True).then_inc(params_in.handle, params_in.unit)
        act.wait_ge(setup_dve, 4)
        for t in range(4):
            a(bias_b[:, t, :], work[:, 1024:1536], ACT.Abs, bias=stat[:, 0, t:t + 1]).then_inc(setup_act, 1)
        for r in range(RES):
            a(work[:, 2048 + 512 * r:2560 + 512 * r], work[:, 1024:1536], ACT.Abs,
              bias=stat[:, 0, 4 + r:5 + r]).then_inc(setup_act, 1)
        a(trig_abs, trig_angle, ACT.Abs).then_inc(setup_act, 1)
        a(trig[:, 0, :, :].rearrange("p t n -> p (t n)"), trig_angle, ACT.Sin).then_inc(setup_act, 1)
        act.wait_ge(setup_dve, 5)
        a(trig[:, 1, :, :].rearrange("p t n -> p (t n)"), trig_abs, ACT.Sin).then_inc(setup_act, 1)
        act.wait_ge(x_in, 16)
        act.wait_ge(rows_clear, 1)
        act.wait_ge(setup_act, 11)

        with layers(act) as l:
            n_ready, n_group, n_unit, n_dve = [0], [0], [0], [0]
            own = Own(act_step)

            def ready():
                n_ready[0] += 1
                act.wait_ge(*pj_ready.at(l, n_ready[0]))
                return PJ[(n_ready[0] - 1) % 4]

            def group():
                n_group[0] += 1
                act.wait_ge(*tp_ready.at(l, n_group[0]))
                return TP[(n_group[0] - 1) % 2]

            L = bass.ds(l, 1)

            def direct(dst, src):
                act.dma_start(dst, src, allow_slow_non_contiguous=True).then_inc(*direct_in.up())

            keep = x_keep.rearrange("(t p) n -> p t n", p=P)

            def staged_squares(width, extra=None, view=lambda s: s):
                for t in range(4):
                    src = ready()
                    if extra is not None:
                        act.wait_ge(*own.done(l))
                        a(*extra(t, src), ACT.Copy).then_inc(*act_step.up(own))
                    act.wait_ge(*own.done(l))
                    a(stage[:, t, 0:width], src[:, 0:width], ACT.Copy).then_inc(*pj_act.up(own))
                    if sq_ready.n >= 2:
                        act.wait_ge(*sq_used.at(l, sq_ready.n - 1))
                    act.wait_ge(*own.done(l))
                    a(view(sq[:, sq_ready.n % 2, 0:width]), view(stage[:, t, 0:width]), ACT.Square).then_inc(*sq_ready.up(own))

            def half_out(dst, gain_of=None, same=None, m=P):
                src = group()
                if same is not None:
                    act.wait_ge(*own.done(l))
                    a(dst(0, 2), src[0:m, 0:2 * P].rearrange("p (c n) -> p c n", c=2), ACT.Copy, scale=same).then_inc(*tp_act.up(own))
                else:
                    for c in range(2):
                        act.wait_ge(*own.done(l))
                        a(dst(c, c + 1), src[0:m, P * c:P * c + P].unsqueeze(1), ACT.Copy, scale=gain_of(c)).then_inc(*(tp_act if c else act_step).up(own))

            def hi_out(dst, gain_col=None):
                kw = {} if gain_col is None else dict(scale=gain_col)
                src = group()
                act.wait_ge(*own.done(l))
                a(dst, src[:, :].rearrange("p (c n) -> p c n", c=4), ACT.Copy, **kw).then_inc(*tp_act.up(own))

            def squares(added):
                for half in range(2):
                    for t in range(4):
                        act.wait_ge(*pj_dve.at(l, added + 4 * half + t + 1))
                        cols = slice(BW * half, BW * half + BW)
                        act.wait_ge(*own.done(l))
                        a(h_sb[:, t, cols], x_sb[:, t, cols], ACT.Square, accum_out=stat[:, 0, 4 * half + t:4 * half + t + 1]).then_inc(*ssum.up(own))

            def norm_out(row):
                g0 = n_group[0]
                for c in range(DC):
                    group()
                    act.wait_ge(*own.done(l))
                    a(hTh[:, c, :], norm_bank(g0, c)[:, :], ACT.Copy, scale=prm[:, row + c:row + c + 1]).then_inc(*tp_act.up(own))

            def exps(u, subs=1, slot=0, with_sink=False, keys=all_keys):
                lo, hi, _mid = keys(u)
                act.wait_ge(*s_biased.at(l, n_unit[0] + u + 1))
                if with_sink:
                    a(stat[:, 11, u:u + 1], sink[:, u % 8:u % 8 + 1], ACT.Exp, scale=-1.0, bias=stat[:, 5, u:u + 1]).then_inc(*act_step.up(own))
                w = P * (hi - lo) // subs
                for r in range(subs):
                    c = u if subs == 1 else 8 * r + u
                    at = P * lo + w * r
                    a(probs[:, u % 2, at:at + w], scores[:, u % 2, at:at + w], ACT.Exp, scale=-1.0, bias=stat[:, 5 + slot, c:c + 1], accum_out=stat[:, 8 + slot, c:c + 1]).then_inc(*(p_ready if r == subs - 1 else act_step).up(own))

            def attention(n, started=0, tile_out=None, keys=all_keys, **kw):
                first = n_unit[0]
                for step in range(started, n + 3):
                    if 2 <= step < n + 2:
                        u = step - 2
                        lo, _hi, mid = keys(u)
                        src = group()
                        if u >= 2:
                            act.wait_ge(*o_ready.at(l, first + u - 1))
                        a(probsT[:, u % 2, P * lo:P * mid], src[:, P * lo:P * mid], ACT.Copy).then_inc(*tp_act.up(own))
                    if step < n:
                        exps(step, keys=keys, **kw)
                    if tile_out and step >= 12 and (step - 12) % 8 == 0:
                        tile_out((step - 12) // 8)
                n_unit[0] += n

            def gates_out():
                act.wait_ge(*pj_dve.at(l, n_dve[0]))
                for m in range(4):
                    src = ready()
                    act.wait_ge(*own.done(l))
                    a(gates[:, m, :], src[:, :], ACT.Tanh, scale=0.5).then_inc(*pj_act.up(own))

            def branch_skipped():
                n_ready[0] += 4
                n_dve[0] += 4

            def gates_and_branch(order, start=lambda: None):
                for cb in range(2):
                    gates_out()
                    if cb == 1:
                        start()
                    branch_skipped()
                if order in (1, 2):
                    act.wait_ge(*merged_sum.at(l, 8 * order))

            def oT(t):
                return gTh[:, 0:4, P * t:P * t + P]

            squares(-8)
            src = group()
            act.wait_ge(*own.done(l))
            a(prm[:, 0:NROW], src[:, 0:NROW], ACT.Copy).then_inc(*act_step.up(own))
            act.wait_ge(*own.done(l))
            a(prm[:, NROW:NROW + 88], src[:, P:P + 88], ACT.Copy).then_inc(*tp_act.up(own))
            norm_out(ROW["norm1"])
            act.dma_start(keep, x_sb).then_inc(*x_moved.up())
            for n, name in enumerate(("d_q_norm", "d_k_norm")):
                direct(rope_rows[:, n, :], io[name][L, NOPE:DQK].broadcast_to([P, ROPE]))
            direct(sink[:], io["a_sink"][L, :].broadcast_to([P, 8]))
            direct(lamc[:], io["k_lam"][L, :].broadcast_to([P, 2]))
            for n, name in enumerate(("b_lam_q1", "b_lam_k1", "b_lam_q2", "b_lam_k2")):
                direct(lam_in[:, n, :], io[name][L].rearrange("a h n -> a (h n)").broadcast_to([P, 256]))
            act.wait_ge(*lam_dot.at(l, 1))
            act.wait_ge(*own.done(l))
            a(lam[:], lam[:], ACT.Exp).then_inc(*lam_exp.up(own))
            act.wait_ge(*x_moved.at(l, 1))
            act.wait_ge(*gains_in.at(l, 1))
            for dst, src in parameter_rows((DEPTH - 1) - l):
                act.dma_start(dst, src, allow_slow_non_contiguous=True).then_inc(*params_in.up())

            for j in range(3):
                staged_squares(512)
                for t in range(4):
                    half_out(lambda c0, c1: qT[:, c0:c1, P * t:P * t + P], lambda c: gain[:, 8 + 4 * j + c:9 + 4 * j + c])
                staged_squares(512)
                for t in range(4):
                    half_out(lambda c0, c1: kT[:, c0:c1, P * t:P * t + P], same=prm[:, ROW["ckn"]:ROW["ckn"] + 1])
                kw = dict(subs=4, slot=j) if j else {}
                for t in range(4):
                    src = ready()
                    act.wait_ge(*own.done(l))
                    a(vB[:, t, :], src[:, :], ACT.Copy).then_inc(*pj_act.up(own))
                    if t < 2:
                        exps(t, **kw)
                attention(8 if j else 32, started=2, **kw)
            act.wait_ge(*c_diff.at(l, 1))
            act.wait_ge(*own.done(l))
            a(stat[:, 12:15, :], stat[:, 12:15, :], ACT.Exp).then_inc(*c_exp.up(own))
            for r in range(RES):
                hi_out(gTh[:, 0:4, :].rearrange("p c (i r) -> p r c i", r=RES)[:, r])

            staged_squares(512, extra=lambda t, src: (vA[:, t, :], src[:, P:2 * P]))
            for t in range(4):
                src = group()
                act.wait_ge(*own.done(l))
                a(kA[:, :, P * t:P * t + P], src[:, 0:256].rearrange("p (c n) -> p c n", c=2), ACT.Copy, scale=prm[:, ROW["ak"]:ROW["ak"] + 1]).then_inc(*act_step.up(own))
                for c in range(2):
                    act.wait_ge(*own.done(l))
                    a(gTh[:, LAT_KV + c, P * t:P * t + P], src[:, 256 + P * c:384 + P * c], ACT.Copy, scale=prm[:, ROW["ckv"] + c:ROW["ckv"] + c + 1]).then_inc(*(tp_act if c else act_step).up(own))
            staged_squares(416)
            for t in range(4):
                src = group()
                for c in range(3):
                    act.wait_ge(*own.done(l))
                    a(gTh[:, LAT_Q + c, P * t:P * t + P], src[:, P * c:P * c + P], ACT.Copy, scale=prm[:, ROW["cq"] + c:ROW["cq"] + c + 1]).then_inc(*(tp_act if c == 2 else act_step).up(own))
            gates_out()
            for hb in range(2):
                staged_squares(384)
                if hb == 0:
                    branch_skipped()
                for t in range(4):
                    half_out(lambda c0, c1: qD[0:DQK, 4 * hb + c0:4 * hb + c1, P * t:P * t + P], same=gain[0:DQK, 21:22], m=DQK)
            gates_out()
            for hb in range(2):
                staged_squares(512, extra=lambda t, src: (
                    vD[:, t, 256 * hb:256 * hb + 256].rearrange("p (h n) -> p h n", h=4),
                    src[:, :].rearrange("p (h n) -> p h n", h=4)[:, :, NOPE:P]),
                    view=lambda s: s.rearrange("p (h n) -> p h n", h=4)[:, :, 0:NOPE])
                if hb == 0:
                    branch_skipped()
                for t in range(4):
                    half_out(lambda c0, c1: kD[0:DQK, 4 * hb + c0:4 * hb + c1, P * t:P * t + P],
                             same=prm[0:DQK, ROW["dk"]:ROW["dk"] + 1], m=DQK)
            attention(32, tile_out=lambda t: hi_out(oT(t)))
            hi_out(oT(3))

            staged_squares(512)
            for t in range(4):
                half_out(lambda c0, c1: qT[:, c0:c1, P * t:P * t + P], lambda c: gain[:, c:c + 1])
            kw = dict(with_sink=True, keys=near_keys)
            gates_and_branch(1, lambda: [exps(u, **kw) for u in range(2)])
            attention(32, started=2, tile_out=lambda t: hi_out(oT(t)), **kw)
            hi_out(oT(3))

            staged_squares(512)
            for t in range(4):
                half_out(lambda c0, c1: qT[:, c0:c1, P * t:P * t + P], lambda c: gain[:, 4 + c:5 + c])
            staged_squares(512)
            for t in range(4):
                half_out(lambda c0, c1: kT[:, c0:c1, P * t:P * t + P], same=prm[:, ROW["bk"]:ROW["bk"] + 1])
            for t in range(4):
                src = ready()
                act.wait_ge(*own.done(l))
                a(vB[:, t, :], src[:, :], ACT.Copy).then_inc(*pj_act.up(own))
            gates_and_branch(2, lambda: [exps(u) for u in range(2)])
            attention(32, started=2)
            act.wait_ge(*o_ready.at(l, n_unit[0]))
            act.wait_ge(*x_moved.at(l, 1))
            act.dma_start(x_sb, keep).then_inc(*x_moved.up())
            for t in range(4):
                hi_out(oT(t), gain[:, 20:21])
            gates_and_branch(3)

            for c in range(DC):
                act.wait_ge(*merged_sum.at(l, 16 + c + 1))
                act.wait_ge(*own.done(l))
                a(hTh[:, c, :], merged[:, c, :], ACT.Copy, scale=0.5).then_inc(*merged_hi.up(own))
            n_ready[0] += 8
            squares(n_dve[0])
            norm_out(ROW["norm2"])
            n_dve[0] += 8

            b = 0
            for size in UP_GROUPS:
                for i in range(size):
                    for m in range(4):
                        src = ready()
                        if m == 0 and b > 0:
                            act.wait_ge(*hidden_lo.at(l, 2 * b))
                        q = 2 * b + m if m < 2 else CONV_B // 2 + 2 * b + m - 2
                        act.wait_ge(*own.done(l))
                        a(hid[:, m, :], src[:, :], ACT.Identity, scale=prm[:, NROW + 44 + q:NROW + 45 + q], bias=prm[:, NROW + 132 + q:NROW + 133 + q]).then_inc(*conv_mid.up(own))
                    for m in range(2):
                        act.wait_ge(*pj_dve.at(l, n_dve[0] + m + 1))
                        act.wait_ge(*own.done(l))
                        a(act_e[:, m, :], hid[:, m, :], ACT.Tanh, scale=0.5).then_inc(*e_ready.up(own))
                    n_dve[0] += 4
                    for m in range(2):
                        act.wait_ge(*hidden_val.at(l, 2 * b + m + 1))
                        act.wait_ge(*own.done(l))
                        a(gTh[:, 2 * i + m, :], act_e[:, m, :], ACT.Copy, scale=0.5).then_inc(*hidden_hi.up(own))
                    b += 1
                n_dve[0] += 8
                n_ready[0] += 8
        act.wait_ge(*params_in.at(DEPTH, 0))

    @block_.vector
    def _(dve):
        v = nc.vector
        setup = [0, 0]

        def su(ins, part=None):
            setup[0] += 1
            ins.then_inc(dve_setup, 1)
            dve.wait_ge(dve_setup, setup[0])

        def publish():
            setup[1] += 1
            v.tensor_copy(lamc[:, 0:1], stat[:, 15, 0:1]).then_inc(setup_dve, 1)
            dve.wait_ge(setup_dve, setup[1])

        dve.wait_ge(setup_in, 16 * 7)
        su(v.memset(stat[:], 0.0))
        su(v.tensor_copy(work[:, 1024:1536], work[:, 512:1024].bitcast(I32)))
        su(v.tensor_copy(stat[:, 1, 0:8], work[:, 256:264].bitcast(I32)))
        su(v.tensor_scalar(stat[:, 0, 0:8], stat[:, 1, 0:8], -1.0, None, ALU.mult))
        for t in range(4):
            su(v.tensor_scalar(trig_angle[:, 16 * t:16 * t + 16], consts[:, 148:164], stat[:, 1, t:t + 1], None, ALU.mult))
        turns = work[:, 1536:1600]
        su(v.tensor_scalar(turns, trig_angle, 1.0 / (2 * math.pi), 12582912.0, ALU.mult, ALU.add))
        su(v.tensor_scalar(turns, turns, 12582912.0, None, ALU.subtract))
        c1 = 6.28125
        c2 = float(np.float32(math.floor((2 * math.pi - c1) * 2 ** 17) / 2 ** 17))
        for c in (c1, c2, 2 * math.pi - c1 - c2):
            su(v.scalar_tensor_tensor(trig_angle, turns, -c, trig_angle, ALU.mult, ALU.add))
        su(v.tensor_scalar(trig_angle, trig_angle, 3.1415925, -3.1415925, ALU.min, ALU.max))
        for _i in range(4):
            publish()
        dve.wait_ge(setup_act, 9)
        su(v.tensor_scalar(trig_abs, trig_abs, -1.0, math.pi / 2, ALU.mult, ALU.add))
        publish()
        su(v.tensor_tensor(bias_a, bias_a, bias_b, ALU.add))
        dist = work[:, 2048:4096].rearrange("p (r n) -> p r n", r=4)
        su(v.tensor_tensor(bias_c0, bias_c0, dist, ALU.add))
        for n in range(2):
            for r in range(RES):
                su(v.tensor_tensor(bias_c12[:, n, P * r:P * r + P], dist[:, r, :].rearrange("p (i r) -> p r i", r=RES)[:, r, :],
                                   work[:, P * n:P * n + P], ALU.add))
        dve.wait_ge(x_in, 16)

        with layers(dve) as l:
            n_ready, n_group, n_unit, n_hi = [0], [0], [0], [0]
            own = Own(pj_dve)

            def ready():
                n_ready[0] += 1
                dve.wait_ge(*pj_ready.at(l, n_ready[0]))
                return PJ[(n_ready[0] - 1) % 4]

            def group():
                n_group[0] += 1
                dve.wait_ge(*tp_ready.at(l, n_group[0]))
                return TP[(n_group[0] - 1) % 2]

            def rsqrt(n, means):
                mean, y, t = stat[:, 1, 0:n], stat[:, 2, 0:n], stat[:, 3, 0:n]
                for lo, hi, width in means:
                    dve.wait_ge(*own.done(l))
                    v.tensor_scalar(stat[:, 1, lo:hi], stat[:, 0, lo:hi], 1.0 / width, EPS, ALU.mult, ALU.add).then_inc(*dve_step.up(own))
                dve.wait_ge(*own.done(l))
                v.tensor_scalar(t.bitcast(I32), mean.bitcast(I32), 1, None, ALU.arith_shift_right).then_inc(*dve_step.up(own))
                dve.wait_ge(*own.done(l))
                v.tensor_scalar(y.bitcast(I32), t.bitcast(I32), -1.0, float(0x5f3759df), ALU.mult, ALU.add).then_inc(*dve_step.up(own))
                for _i in range(3):
                    dve.wait_ge(*own.done(l))
                    v.tensor_tensor(t, y, y, ALU.mult).then_inc(*dve_step.up(own))
                    dve.wait_ge(*own.done(l))
                    v.scalar_tensor_tensor(t, t, -0.5, mean, ALU.mult, ALU.mult).then_inc(*dve_step.up(own))
                    dve.wait_ge(*own.done(l))
                    v.scalar_tensor_tensor(y, t, 1.5, y, ALU.add, ALU.mult).then_inc(*dve_step.up(own))

            def sums(outs, n=4):
                for t in range(4):
                    dve.wait_ge(*sq_ready.at(l, sq_used.n + 1))
                    parts = outs(t, sq[:, sq_used.n % 2, :])
                    for k, (dst, src) in enumerate(parts):
                        dve.wait_ge(*own.done(l))
                        v.tensor_reduce(dst, src, AXX, ALU.add).then_inc(*(sq_used if k == len(parts) - 1 else dve_step).up(own))

            def heads(ap, h, w=None):
                return ap.rearrange("p (h n) -> p h n", h=h)

            def over(col, n):
                return col.unsqueeze(2).to_broadcast([P, col.shape[1], n])

            def head_norm():
                sums(lambda t, s: [(stat[:, 0, 8 * t:8 * t + 8], heads(s, 8))])
                rsqrt(32, [(0, 32, HD)])
                for t in range(4):
                    dve.wait_ge(*own.done(l))
                    v.tensor_tensor(heads(stage[:, t, :], 8), heads(stage[:, t, :], 8), over(stat[:, 2, 8 * t:8 * t + 8], HD), ALU.mult).then_inc(*normed.up(own))

            def half_out(dst, gain_of=None, same=None, m=P):
                src = group()
                dve.wait_ge(*tp_act.at(l, n_group[0]))
                if same is not None:
                    dve.wait_ge(*own.done(l))
                    v.tensor_scalar(dst(2, 4), src[0:m, 2 * P:4 * P].rearrange("p (c n) -> p c n", c=2), same, None, ALU.mult).then_inc(*tp_dve.up(own))
                else:
                    for c in (2, 3):
                        dve.wait_ge(*own.done(l))
                        v.tensor_scalar(dst(c, c + 1), src[0:m, P * c:P * c + P].unsqueeze(1), gain_of(c), None, ALU.mult).then_inc(*(tp_dve if c == 3 else dve_step).up(own))

            def lo_out(lo, hi, gain_col=1.0):
                src = group()
                dve.wait_ge(*tp_act.at(l, n_group[0]))
                dve.wait_ge(*own.done(l))
                v.scalar_tensor_tensor(lo, src[:, :].rearrange("p (c n) -> p c n", c=4), gain_col, hi.bitcast(F32), ALU.mult, ALU.subtract).then_inc(*tp_dve.up(own))

            def normalise():
                dve.wait_ge(*ssum.at(l, n_hi[0] + 8))
                n_hi[0] += 8
                dve.wait_ge(*own.done(l))
                v.tensor_tensor(stat[:, 0, 0:4], stat[:, 0, 0:4], stat[:, 0, 4:8], ALU.add).then_inc(*dve_step.up(own))
                rsqrt(4, [(0, 4, DM)])
                for t in range(4):
                    if t == 0:
                        dve.wait_ge(*own.done(l))
                    v.tensor_scalar(h_sb[:, t, :], x_sb[:, t, :], stat[:, 2, t:t + 1], None, ALU.mult).then_inc(*normed.up(own))

            def norm_out(row):
                g0 = n_group[0]
                for c in range(DC):
                    group()
                    src = norm_bank(g0, c)
                    dve.wait_ge(*tp_act.at(l, n_group[0]))
                    v.scalar_tensor_tensor(hTl[:, c, :], src[:, :], prm[:, row + c:row + c + 1], hTh[:, c, :].bitcast(F32), ALU.mult, ALU.subtract).then_inc(*tp_dve.up(own))

            def bias_step(u, biased):
                dve.wait_ge(*s_ready.at(l, n_unit[0] + u + 1))
                if u >= 2:
                    dve.wait_ge(*p_ready.at(l, n_unit[0] + u - 1))
                biased(u, SB[u % 2], scores[:, u % 2, :])

            def attention(n, biased, out, started=0, keys=all_keys, tile_out=None):
                first = n_unit[0]
                for step in range(started, n + 3):
                    if step < n:
                        bias_step(step, biased)
                    if 2 <= step < n + 2:
                        u = step - 2
                        _lo, hi, mid = keys(u)
                        src = group()
                        if u >= 2:
                            dve.wait_ge(*o_ready.at(l, first + u - 1))
                        dve.wait_ge(*tp_act.at(l, n_group[0]))
                        v.tensor_copy(probsT[:, u % 2, P * mid:P * hi], src[:, P * mid:P * hi]).then_inc(*tp_dve.up(own))
                    if step >= 3:
                        u = step - 3
                        dve.wait_ge(*o_ready.at(l, first + u + 1))
                        out(u, OB[u % 2][:, 0:256])
                    if tile_out and step >= 12 and (step - 12) % 8 == 0:
                        tile_out((step - 12) // 8)
                n_unit[0] += n

            def biased_dense(bias_t, slopes, floor=None, head=lambda u: u % 8, keys=all_keys):
                def biased(u, src, dst):
                    lo, hi, _mid = keys(u)
                    cols = slice(P * lo, P * hi)
                    start = MASKED if floor is None else floor(u)
                    dve.sem_inc(waits_met, 1)
                    v.tensor_tensor_reduce(out=dst[:, cols], in0=src[:, cols], in1=bias_t[:, u // 8, cols], scale=slopes[head(u)], scalar=start, accum_out=stat[:, 5, u:u + 1], op0=ALU.add, op1=ALU.min).then_inc(*s_biased.up(own))
                return biased

            def keep_outputs(u, src):
                t, h = u // 8, u % 8
                v.tensor_copy(otok[:, t % 2, HD * h:HD * h + HD], src[:, 0:HD]).then_inc(*o_out.up(own))

            def dense_out(with_sink=False):
                def out(u, src):
                    keep_outputs(u, src)
                    if u % 8 < 7:
                        return
                    t = u // 8
                    den = stat[:, 8, 8 * t:8 * t + 8]
                    if with_sink:
                        dve.wait_ge(*own.done(l))
                        v.tensor_tensor(den, den, stat[:, 11, 8 * t:8 * t + 8], ALU.add).then_inc(*dve_step.up(own))
                    dve.wait_ge(*own.done(l))
                    v.reciprocal(stat[:, 4, 16:24], den).then_inc(*dve_step.up(own))
                    o = heads(otok[:, t % 2, :], 8)
                    dve.wait_ge(*own.done(l))
                    v.tensor_tensor(o, o, over(stat[:, 4, 16:24], HD), ALU.mult).then_inc(*normed.up(own))
                return out

            def tile_steps(t, gain_col=1.0):
                lo_out(gTl[:, 0:4, P * t:P * t + P], gTh[:, 0:4, P * t:P * t + P], gain_col)

            def gates_skipped():
                n_ready[0] += 4
                n_act[0] += 4

            def branch_out(order, cb):
                dve.wait_ge(*pj_act.at(l, n_act[0]))
                for m in range(4):
                    src = ready()
                    c = 4 * cb + m
                    dst = merged[:, c, :] if order == 0 else branch_tmp[:, m % 2, :]
                    dve.wait_ge(*own.done(l))
                    v.scalar_tensor_tensor(dst, gates[:, m, :], 1.0, src[:, :], ALU.add, ALU.mult).then_inc(*pj_dve.up(own))
                    if order:
                        dve.wait_ge(*own.done(l))
                        v.tensor_tensor(merged[:, c, :], merged[:, c, :], dst, ALU.add).then_inc(*merged_sum.up(own))

            def gates_and_branch(order, start=lambda: None):
                for cb in range(2):
                    gates_skipped()
                    if cb == 1:
                        start()
                    if cb == 1 and order == 3:
                        for c in range(4):
                            merged_split(c)
                    branch_out(order, cb)

            def merged_split(c):
                dve.wait_ge(*merged_hi.at(l, c + 1))
                dve.wait_ge(*own.done(l))
                v.scalar_tensor_tensor(hTl[:, c, :], merged[:, c, :], 0.5, hTh[:, c, :].bitcast(F32), ALU.mult, ALU.subtract).then_inc(*merged_lo.up(own))

            n_act = [0]

            normalise()
            dve.wait_ge(*params_in.at(l, 0))
            src = group()
            dve.wait_ge(*tp_act.at(l, 1))
            dve.wait_ge(*own.done(l))
            v.tensor_copy(prm[:, NROW + 88:NROW + 176], src[:, 256:344]).then_inc(*tp_dve.up(own))
            dve.wait_ge(*tp_act.at(l, 1))
            for at, n, key in ((0, 4, "aq"), (4, 4, "bq"), (8, 12, "cqn")):
                dve.wait_ge(*own.done(l))
                v.tensor_scalar(gain[:, at:at + n], consts[:, 128 + at:128 + at + n], prm[:, ROW[key]:ROW[key] + 1], None, ALU.mult).then_inc(*dve_step.up(own))
            dve.wait_ge(*own.done(l))
            v.tensor_scalar(gain[:, 21:22], prm[:, ROW["dq"]:ROW["dq"] + 1], -DQK ** -0.5, None, ALU.mult).then_inc(*dve_step.up(own))
            norm_out(ROW["norm1"])
            dve.wait_ge(*direct_in.at(l, direct_in.each))
            dve.wait_ge(*own.done(l))
            v.tensor_scalar(gain[:, 20:21], prm[:, ROW["subln"]:ROW["subln"] + 1], lamc[:, 1:2], None, ALU.mult).then_inc(*dve_step.up(own))
            dve.wait_ge(*own.done(l))
            v.tensor_scalar(sink[:], sink[:], -1.0, None, ALU.mult).then_inc(*gains_in.up(own))
            for n in range(2):
                dve.wait_ge(*own.done(l))
                v.tensor_tensor(lam_in[:, 2 * n, :], lam_in[:, 2 * n, :], lam_in[:, 2 * n + 1, :], ALU.mult).then_inc(*dve_step.up(own))
                dve.wait_ge(*own.done(l))
                v.tensor_reduce(lam[:, 4 * n:4 * n + 4], heads(lam_in[:, 2 * n, :], 4), AXX, ALU.add).then_inc(*(lam_dot if n else dve_step).up(own))
            dve.wait_ge(*lam_exp.at(l, 1))
            dve.wait_ge(*own.done(l))
            v.scalar_tensor_tensor(lam[:, 0:4], lam[:, 4:8], lamc[:, 0:1], lam[:, 0:4], ALU.subtract, ALU.subtract).then_inc(*dve_step.up(own))
            dve.wait_ge(*x_moved.at(l, 1))

            for j in range(3):
                head_norm()
                for t in range(4):
                    half_out(lambda c0, c1: qT[:, c0:c1, P * t:P * t + P], lambda c: gain[:, 8 + 4 * j + c:9 + 4 * j + c])
                head_norm()
                for t in range(4):
                    half_out(lambda c0, c1: kT[:, c0:c1, P * t:P * t + P], same=prm[:, ROW["ckn"]:ROW["ckn"] + 1])
                n_ready[0] += 12
                n_act[0] += 12
                if j == 0:
                    def keep(u, src):
                        v.tensor_copy(oC[:, 0, u // 8, HD * (u % 8):HD * (u % 8) + HD], src[:, 0:HD]).then_inc(*o_out.up(own))
                    biased = biased_dense(bias_c0, C_SLOPES[0])
                else:
                    def biased(h, src, dst):
                        for r in range(RES):
                            dve.sem_inc(waits_met, 1)
                            v.tensor_tensor_reduce(out=dst[:, P * r:P * r + P], in0=src[:, P * r:P * r + P], in1=bias_c12[:, j - 1, P * r:P * r + P], scale=C_SLOPES[j][h], scalar=MASKED, accum_out=stat[:, 5 + j, 8 * r + h:8 * r + h + 1], op0=ALU.add, op1=ALU.min).then_inc(*(s_biased if r == 3 else dve_step).up(own))

                    def keep(h, src):
                        v.tensor_copy(oC[:, j, :, HD * h:HD * h + HD], heads(src, 4)).then_inc(*o_out.up(own))
                for u in range(2):
                    bias_step(u, biased)
                attention(8 if j else 32, biased, keep, started=2)
            dve.wait_ge(*own.done(l))
            v.tensor_tensor(stat[:, 15, :], stat[:, 5, :], stat[:, 6, :], ALU.min).then_inc(*dve_step.up(own))
            dve.wait_ge(*own.done(l))
            v.tensor_tensor(stat[:, 15, :], stat[:, 15, :], stat[:, 7, :], ALU.min).then_inc(*dve_step.up(own))
            for j in range(3):
                dve.wait_ge(*own.done(l))
                v.tensor_tensor(stat[:, 12 + j, :], stat[:, 15, :], stat[:, 5 + j, :], ALU.subtract).then_inc(*(c_diff if j == 2 else dve_step).up(own))
            dve.wait_ge(*c_exp.at(l, 1))
            dve.wait_ge(*own.done(l))
            v.tensor_tensor(stat[:, 8:11, :], stat[:, 8:11, :], stat[:, 12:15, :], ALU.mult).then_inc(*dve_step.up(own))
            dve.wait_ge(*own.done(l))
            v.tensor_tensor(stat[:, 8, :], stat[:, 8, :], stat[:, 9, :], ALU.add).then_inc(*dve_step.up(own))
            dve.wait_ge(*own.done(l))
            v.tensor_tensor(stat[:, 8, :], stat[:, 8, :], stat[:, 10, :], ALU.add).then_inc(*dve_step.up(own))
            dve.wait_ge(*own.done(l))
            v.reciprocal(stat[:, 8, :], stat[:, 8, :]).then_inc(*dve_step.up(own))
            for j in range(3):
                dve.wait_ge(*own.done(l))
                v.tensor_tensor(stat[:, 12 + j, :], stat[:, 12 + j, :], stat[:, 8, :], ALU.mult).then_inc(*dve_step.up(own))
            for t in range(4):
                for j in range(3):
                    o = oC[:, j, t, :]
                    dve.wait_ge(*own.done(l))
                    v.tensor_tensor(heads(o, 8), heads(o, 8), over(stat[:, 12 + j, 8 * t:8 * t + 8], HD), ALU.mult).then_inc(*dve_step.up(own))
                    if j:
                        dve.wait_ge(*own.done(l))
                        v.tensor_tensor(oC[:, 0, t, :], oC[:, 0, t, :], o, ALU.add).then_inc(*(normed if j == 2 else dve_step).up(own))
            for r in range(RES):
                lo_out(gTl[:, 0:4, :].rearrange("p c (i r) -> p r c i", r=RES)[:, r],
                       gTh[:, 0:4, :].rearrange("p c (i r) -> p r c i", r=RES)[:, r])

            sums(lambda t, s: [(stat[:, 0, 2 * t:2 * t + 2], heads(s[:, 0:P], 2)), (stat[:, 0, 8 + t:9 + t], s[:, 256:512])])
            rsqrt(12, [(0, 8, HD), (8, 12, KVR)])
            for t in range(4):
                for dup in range(2):
                    dve.wait_ge(*own.done(l))
                    v.tensor_tensor(kdup[:, t, :].rearrange("p (g d n) -> p g d n", g=2, d=2)[:, :, dup, :], heads(stage[:, t, 0:P], 2), over(stat[:, 2, 2 * t:2 * t + 2], HD), ALU.mult).then_inc(*dve_step.up(own))
                dve.wait_ge(*own.done(l))
                v.tensor_scalar(stage[:, t, 256:512], stage[:, t, 256:512], stat[:, 2, 8 + t:9 + t], None, ALU.mult).then_inc(*normed.up(own))
            for t in range(4):
                src = group()
                dve.wait_ge(*tp_act.at(l, n_group[0]))
                for c in range(2):
                    dve.wait_ge(*own.done(l))
                    v.scalar_tensor_tensor(gTl[:, LAT_KV + c, P * t:P * t + P], src[:, 256 + P * c:384 + P * c], prm[:, ROW["ckv"] + c:ROW["ckv"] + c + 1], gTh[:, LAT_KV + c, P * t:P * t + P].bitcast(F32), ALU.mult, ALU.subtract).then_inc(*(tp_dve if c else dve_step).up(own))
            n_ready[0] += 4
            n_act[0] += 4

            def rope(out1, out2, x1, x2, cos, sin, tmp1, tmp2, last=dve_step):
                tt = v.tensor_tensor
                dve.wait_ge(*own.done(l))
                tt(tmp1, x1, sin, ALU.mult).then_inc(*dve_step.up(own))
                dve.wait_ge(*own.done(l))
                tt(tmp2, x2, sin, ALU.mult).then_inc(*dve_step.up(own))
                dve.wait_ge(*own.done(l))
                tt(x1, x1, cos, ALU.mult).then_inc(*dve_step.up(own))
                dve.wait_ge(*own.done(l))
                tt(x2, x2, cos, ALU.mult).then_inc(*dve_step.up(own))
                dve.wait_ge(*own.done(l))
                tt(out1, x1, tmp2, ALU.subtract).then_inc(*dve_step.up(own))
                dve.wait_ge(*own.done(l))
                tt(out2, x2, tmp1, ALU.add).then_inc(*last.up(own))

            sums(lambda t, s: [(stat[:, 0, t:t + 1], s[:, 0:QR]), (stat[:, 4, 8 + t:9 + t], s[:, QR:QR + ROPE])])
            rsqrt(4, [(0, 4, QR)])
            for t in range(4):
                dve.wait_ge(*own.done(l))
                v.tensor_tensor(krr[:, t, :], stage[:, t, QR:QR + ROPE], rope_rows[:, 1, :], ALU.mult).then_inc(*dve_step.up(own))
                dve.wait_ge(*own.done(l))
                v.tensor_scalar(stage[:, t, 0:QR], stage[:, t, 0:QR], stat[:, 2, t:t + 1], None, ALU.mult).then_inc(*normed.up(own))
            rt = [rope_tmp[:, 64 * n:64 * n + 64].rearrange("p (t n) -> p t n", t=4) for n in range(2)]
            rope(krr[:, :, 0:16], krr[:, :, 16:32], krr[:, :, 0:16], krr[:, :, 16:32], trig[:, 1, :, :], trig[:, 0, :, :], *rt)
            for t in range(4):
                src = group()
                dve.wait_ge(*tp_act.at(l, n_group[0]))
                for c in range(3):
                    dve.wait_ge(*own.done(l))
                    v.scalar_tensor_tensor(gTl[:, LAT_Q + c, P * t:P * t + P], src[:, P * c:P * c + P], prm[:, ROW["cq"] + c:ROW["cq"] + c + 1], gTh[:, LAT_Q + c, P * t:P * t + P].bitcast(F32), ALU.mult, ALU.subtract).then_inc(*(tp_dve if c == 2 else dve_step).up(own))
            n_ready[0] += 4
            n_act[0] += 4
            gates_skipped()
            for hb in range(2):
                sums(lambda t, s: [(stat[:, 0, 4 * t:4 * t + 4], heads(s[:, 0:384], 4))])
                rsqrt(16, [(0, 16, DQK)])
                for t in range(4):
                    q = heads(stage[:, t, 0:384], 4)
                    dve.wait_ge(*own.done(l))
                    v.tensor_tensor(q, q, over(stat[:, 2, 4 * t:4 * t + 4], DQK), ALU.mult).then_inc(*dve_step.up(own))
                rot = stage[:, :, 0:384].rearrange("p t (h n) -> p t h n", h=4)[:, :, :, NOPE:DQK]
                dve.wait_ge(*own.done(l))
                v.tensor_tensor(rot, rot, rope_rows[:, 0:1, :].unsqueeze(1).to_broadcast([P, 4, 4, ROPE]), ALU.mult).then_inc(*dve_step.up(own))
                cs = [trig[:, n, :, :].unsqueeze(2).to_broadcast([P, 4, 4, 16]) for n in (1, 0)]
                tmp = [rope_tmp[:, 256 * n:256 * n + 256].rearrange("p (t h n) -> p t h n", t=4, h=4) for n in range(2)]
                rope(rot[:, :, :, 0:16], rot[:, :, :, 16:32], rot[:, :, :, 0:16], rot[:, :, :, 16:32], *cs, *tmp, last=normed)
                n_ready[0] += 4
                n_act[0] += 4
                if hb == 0:
                    branch_out(0, 0)
                for t in range(4):
                    half_out(lambda c0, c1: qD[0:DQK, 4 * hb + c0:4 * hb + c1, P * t:P * t + P], same=gain[0:DQK, 21:22], m=DQK)
            gates_skipped()
            for hb in range(2):
                sums(lambda t, s: [(stat[:, 0, 4 * t:4 * t + 4], heads(s, 4)[:, :, 0:NOPE])])
                for t in range(4):
                    dve.wait_ge(*own.done(l))
                    v.tensor_scalar(stat[:, 0, 4 * t:4 * t + 4], stat[:, 0, 4 * t:4 * t + 4], stat[:, 4, 8 + t:9 + t], None, ALU.add).then_inc(*dve_step.up(own))
                rsqrt(16, [(0, 16, DQK)])
                for t in range(4):
                    k = heads(stage[:, t, :], 4)
                    dve.wait_ge(*own.done(l))
                    v.tensor_tensor(k[:, :, 0:NOPE], k[:, :, 0:NOPE], over(stat[:, 2, 4 * t:4 * t + 4], NOPE), ALU.mult).then_inc(*dve_step.up(own))
                    dve.wait_ge(*own.done(l))
                    v.tensor_tensor(k[:, :, NOPE:DQK], krr[:, t:t + 1, :].to_broadcast([P, 4, ROPE]), over(stat[:, 2, 4 * t:4 * t + 4], ROPE), ALU.mult).then_inc(*normed.up(own))
                n_ready[0] += 4
                n_act[0] += 4
                if hb == 0:
                    branch_out(0, 1)
                for t in range(4):
                    half_out(lambda c0, c1: kD[0:DQK, 4 * hb + c0:4 * hb + c1, P * t:P * t + P],
                             same=prm[0:DQK, ROW["dk"]:ROW["dk"] + 1], m=DQK)

            def biased_d(u, src, dst):
                v.tensor_scalar(dst, src[:, :], 1.0, MASKED, ALU.mult, ALU.min, accum_out=stat[:, 5, u:u + 1]).then_inc(*s_biased.up(own))

            attention(32, biased_d, dense_out(), tile_out=tile_steps)
            tile_steps(3)

            head_norm()
            for t in range(4):
                half_out(lambda c0, c1: qT[:, c0:c1, P * t:P * t + P], lambda c: gain[:, c:c + 1])
            n_ready[0] += 4
            n_act[0] += 4
            biased = biased_dense(bias_a, A_SLOPES, floor=lambda u: sink[:, u % 8:u % 8 + 1], keys=near_keys)
            gates_and_branch(1, lambda: [bias_step(u, biased) for u in range(2)])
            attention(32, biased, dense_out(with_sink=True), started=2, keys=near_keys, tile_out=tile_steps)
            tile_steps(3)

            head_norm()
            for t in range(4):
                half_out(lambda c0, c1: qT[:, c0:c1, P * t:P * t + P], lambda c: gain[:, 4 + c:5 + c])
            head_norm()
            for t in range(4):
                half_out(lambda c0, c1: kT[:, c0:c1, P * t:P * t + P], same=prm[:, ROW["bk"]:ROW["bk"] + 1])
            n_ready[0] += 12
            n_act[0] += 12
            biased = biased_dense(bias_b, B_SLOPES, head=lambda u: (u % 8) // 2)
            gates_and_branch(2, lambda: [bias_step(u, biased) for u in range(2)])

            def out_b(u, src):
                t, h, m = u // 8, (u % 8) // 2, u % 2
                o = oB[:, t, P * h:P * h + P]
                dve.wait_ge(*own.done(l))
                v.reciprocal(stat[:, 4, 0:1], stat[:, 8, u:u + 1]).then_inc(*dve_step.up(own))
                if m == 0:
                    dve.wait_ge(*own.done(l))
                    v.tensor_scalar(o, src[:, 0:P], stat[:, 4, 0:1], None, ALU.mult).then_inc(*o_out.up(own))
                else:
                    dve.wait_ge(*own.done(l))
                    v.tensor_tensor(stat[:, 4, 0:1], stat[:, 4, 0:1], lam[:, h:h + 1], ALU.mult).then_inc(*dve_step.up(own))
                    dve.wait_ge(*own.done(l))
                    v.scalar_tensor_tensor(o, src[:, 0:P], stat[:, 4, 0:1], o, ALU.mult, ALU.add).then_inc(*o_out.up(own))

            attention(32, biased, out_b, started=2)
            for t in range(4):
                dve.wait_ge(*own.done(l))
                v.tensor_tensor(sq[:, t % 2, :], oB[:, t, :], oB[:, t, :], ALU.mult).then_inc(*dve_step.up(own))
                dve.wait_ge(*own.done(l))
                v.tensor_reduce(stat[:, 0, 4 * t:4 * t + 4], heads(sq[:, t % 2, :], 4), AXX, ALU.add).then_inc(*dve_step.up(own))
            rsqrt(16, [(0, 16, P)])
            for t in range(4):
                o = heads(oB[:, t, :], 4)
                dve.wait_ge(*own.done(l))
                v.tensor_tensor(o, o, over(stat[:, 2, 4 * t:4 * t + 4], P), ALU.mult).then_inc(*normed.up(own))
            for t in range(4):
                tile_steps(t, gain[:, 20:21])
            gates_and_branch(3)

            for c in range(4, DC):
                merged_split(c)
            dve.wait_ge(*x_moved.at(l, 2))

            def add_to_x():
                for cb in range(2):
                    for t in range(4):
                        src = ready()
                        xs = x_sb[:, t, BW * cb:BW * cb + BW]
                        dve.wait_ge(*own.done(l))
                        v.tensor_tensor(xs, src[:, :], xs, ALU.add).then_inc(*pj_dve.up(own))

            add_to_x()
            normalise()
            norm_out(ROW["norm2"])

            b = 0
            for size in UP_GROUPS:
                for i in range(size):
                    for m in range(4):
                        src = ready()
                        q = 2 * b + m if m < 2 else CONV_B // 2 + 2 * b + m - 2
                        dve.wait_ge(*conv_mid.at(l, 4 * b + m + 1))
                        y = hid[:, m, :]
                        dve.wait_ge(*own.done(l))
                        v.scalar_tensor_tensor(y[:, 1:SEQ], src[:, 0:SEQ - 1], prm[:, NROW + q:NROW + 1 + q], y[:, 1:SEQ], ALU.mult, ALU.add).then_inc(*dve_step.up(own))
                        dve.wait_ge(*own.done(l))
                        v.scalar_tensor_tensor(y[:, 0:SEQ - 1], src[:, 1:SEQ], prm[:, NROW + 88 + q:NROW + 89 + q], y[:, 0:SEQ - 1], ALU.mult, ALU.add).then_inc(*pj_dve.up(own))
                    for m in range(2):
                        e = act_e[:, m, :]
                        dve.wait_ge(*e_ready.at(l, 2 * b + m + 1))
                        dve.wait_ge(*own.done(l))
                        v.scalar_tensor_tensor(e, e, 1.0, hid[:, m, :], ALU.add, ALU.mult).then_inc(*dve_step.up(own))
                        dve.wait_ge(*own.done(l))
                        v.tensor_tensor(e, e, hid[:, 2 + m, :], ALU.mult).then_inc(*hidden_val.up(own))
                    for m in range(2):
                        dve.wait_ge(*hidden_hi.at(l, 2 * b + m + 1))
                        dve.wait_ge(*own.done(l))
                        v.scalar_tensor_tensor(gTl[:, 2 * i + m, :], act_e[:, m, :], 0.5, gTh[:, 2 * i + m, :].bitcast(F32), ALU.mult, ALU.subtract).then_inc(*hidden_lo.up(own))
                    b += 1
                add_to_x()

    for name, s in signals.items():
        if s.n != s.each:
            wrong[name] = s.n
    assert not wrong, f"increments in a layer: {wrong}"


_INS = ["x", "positions", "norm1_g", "w_in", "a_q_norm", "a_k_norm", "a_sink", "b_q_norm", "b_k_norm", "b_lam_q1",
        "b_lam_k1", "b_lam_q2", "b_lam_k2", "b_subln_g", "c_q_norm", "c_k_norm", "d_cq_norm", "d_ckv_norm", "d_w_uq",
        "d_w_ukv", "d_q_norm", "d_k_norm", "w_branch", "w_o", "norm2_g", "ffn_w_up", "ffn_conv_w", "ffn_conv_b",
        "ffn_w_down"]


def kernel(**inputs):
    import numpy as _np
    import concourse.bacc as _bacc
    from concourse import mybir as _mybir
    from concourse.bass_utils import run_bass_kernel_spmd as _run

    nc = _bacc.Bacc("TRN2", target_bir_lowering=False, num_devices=1)
    arrays, io = {}, {}
    given = {name: _np.ascontiguousarray(inputs[name]) for name in _INS}
    given.update(shape_constants())
    for name, a in given.items():
        arrays[f"in_{name}"] = a
        io[name] = nc.dram_tensor(f"in_{name}", a.shape, _mybir.dt.from_np(a.dtype), kind="ExternalInput").ap()
    io["y"] = nc.dram_tensor("out_y", (1, SEQ, DM), _mybir.dt.from_np(_np.dtype("float32")), kind="ExternalOutput").ap()
    build(nc, io)
    return _run(nc, [arrays], core_ids=[0]).results[0]["out_y"]
```

```python
import math
from contextlib import ExitStack

import numpy as np
import concourse.bass as bass
from concourse import mybir

F32 = mybir.dt.float32
F32R = mybir.dt.float32r
I32 = mybir.dt.int32
ALU = mybir.AluOpType
ACT = mybir.ActivationFunctionType
AXX = mybir.AxisListType.X

P = 128
DM, SEQ, DEPTH = 1024, 512, 2
TT = SEQ // P
DC = DM // P
HD = 64
FF = 2816
BW = 512
A_RADIUS = 128
C_PATTERNS = ((128, 1), (512, 4), (2048, 16))
RES = 4
QR, KVR, NOPE, ROPE, DV = 384, 256, 64, 32, 64
DQK = NOPE + ROPE
EPS = 1e-6
MASKED = 1e30
SCALE = HD ** -0.5
COL = dict(Aq=0, Akv=512, B=768, C=2304, cq=6912, ckv=7296, kr=7552, gate=7584)
LAT_Q, LAT_KV = 4, 7
HALF = 384 * 3
UP_GROUPS = (4, 4, 3)

ROW = dict(norm1=0, norm2=8, cq=16, ckv=19, subln=21, aq=22, ak=23, bq=24, bk=25, cqn=26, ckn=27, dq=28, dk=29)
NROW = 30
CONV_B = FF * 2 // P

A_SLOPES = [2.0 ** (-8.0 * (i + 1) / 8) for i in range(8)]
B_SLOPES = [2.0 ** (-8.0 * (i + 1) / 4) for i in range(4)]
C_SLOPES = [[2.0 ** (-8.0 * (j * 8 + i + 1) / 24) for i in range(8)] for j in range(3)]


def shape_constants():
    i = np.arange(P)[:, None, None]
    t = np.arange(TT)[None, :, None]
    j = np.arange(SEQ)[None, None, :]
    mask_a = np.where(np.abs(P * t + i - j) <= A_RADIUS, 0.0, MASKED)
    mask_c0 = np.where(np.abs(P * t + i - j) <= C_PATTERNS[0][0] // 2, 0.0, MASKED)
    q, k = np.arange(P)[:, None], np.arange(P)[None, :]
    mask_c1 = np.where(np.abs(q - k) <= C_PATTERNS[1][0] // 8, 0.0, MASKED)
    mask_c2 = np.where((q - k) % 4 == 0, 0.0, MASKED)
    consts = np.zeros((P, 128 + 20 + 16), np.float32)
    consts[:, :P] = np.eye(P)
    for c in range(4):
        for half in range(2):
            rows = slice(64 * half, 64 * half + 64)
            h = 2 * c + half
            consts[rows, 128 + c] = -SCALE / A_SLOPES[h]
            consts[rows, 132 + c] = -SCALE / B_SLOPES[h % 4]
            for n in range(3):
                consts[rows, 136 + 4 * n + c] = -SCALE / C_SLOPES[n][h]
    consts[:, 148:164] = 10000.0 ** (-np.arange(16, dtype=np.float32) / np.float32(16))
    lam = np.array([[0.8 - 0.6 * math.exp(-0.3 * n), 0.2 + 0.6 * math.exp(-0.3 * n)] for n in range(DEPTH)])
    return dict(
        k_mask_a=mask_a.astype(np.float32), k_mask_c0=mask_c0.astype(np.float32),
        k_mask_c12=np.stack([mask_c1, mask_c2], 1).astype(np.float32),
        k_consts=consts, k_lam=lam.astype(np.float32),
    )


class Signal:

    def __init__(self, handle, before, each, unit=1):
        self.handle, self.before, self.each, self.unit, self.n = handle, before, each, unit, 0

    def at(self, layer, k):
        return self.handle, self.unit * (layer * self.each + self.before + k)

    def up(self, own=None):
        self.n += 1
        if own is not None:
            own.last, own.k = self, self.n
        return self.handle, self.unit


class Own:

    def __init__(self, last, k=0):
        self.last, self.k = last, k

    def done(self, layer):
        return self.last.at(layer, self.k)


EACH = dict(
    raw_landed0=119, raw_landed1=119, hi_split=186, tile_split=186, tile_used=132, pj_ready=216, pj_act=108,
    pj_dve=108, sq_used=60, normed=78, tp_ready=237, tp_act=237, tp_dve=237, s_ready=144,
    s_biased=144, p_ready=144, o_ready=144, o_out=144, gains_in=1, ssum=16, lam_dot=1, lam_exp=1, c_diff=1,
    c_exp=1, merged_sum=24, merged_hi=8, merged_lo=8, conv_mid=44, e_ready=22, hidden_val=22, hidden_hi=22,
    hidden_lo=22, act_step=189, dve_step=525, params_in=16, direct_in=8, x_moved=2, c0_moved=6,
)


def build(nc, io):
    ctx = ExitStack()
    with ctx:
        _build(nc, io, ctx)


def _build(nc, io, ctx):
    def sb(name, shape, dt=F32):
        return ctx.enter_context(nc.sbuf_tensor("s_" + name, shape, dt))

    signals, wrong = {}, {}

    def signal(name, before=0, unit=1):
        s = Signal(ctx.enter_context(nc.semaphore(name)), before, EACH.get(name, 0), unit)
        signals[name] = s
        return s

    def sem(name):
        return ctx.enter_context(nc.semaphore(name))

    hTh, hTl = sb("hTh", [P, DC, SEQ], F32R), sb("hTl", [P, DC, SEQ], F32R)
    gTh, gTl = sb("gTh", [P, DC + 1, SEQ], F32R), sb("gTl", [P, DC + 1, SEQ], F32R)
    raw = sb("raw", [P, 2, HALF])
    wh, wl = sb("wh", [P, 2, HALF], F32R), sb("wl", [P, 2, HALF], F32R)
    bias = sb("bias", [P, 14, SEQ])
    work = sb("work", [P, 19968])
    consts = sb("consts", [P, 164])
    rows = sb("rows", [P, 3, P])
    prm = sb("prm", [P, NROW + 4 * CONV_B])
    gain = sb("gain", [P, 24])
    rope_rows = sb("rope_rows", [P, 2, ROPE])
    trig = sb("trig", [P, 2, TT, 16])
    sink = sb("sink", [P, 8])
    one = sb("one", [P, 1])
    lamc = sb("lamc", [P, 2])
    lam = sb("lam", [P, 8])
    stat = sb("stat", [P, 16, 32])
    krr = sb("krr", [P, TT, ROPE])

    ident = consts[:, 0:P]
    bias_a, bias_b, bias_c0 = bias[:, 0:4, :], bias[:, 4:8, :], bias[:, 8:12, :]
    bias_c12 = bias[:, 12:14, :]
    stage = work[:, 0:2048].rearrange("p (t n) -> p t n", t=4)
    sq = work[:, 2048:3072].rearrange("p (s n) -> p s n", s=2)
    kdup = work[:, 3072:4096].rearrange("p (t n) -> p t n", t=4)
    scores = work[:, 0:1024].rearrange("p (s n) -> p s n", s=2)
    probs = work[:, 1024:2048].rearrange("p (s n) -> p s n", s=2)
    probsT = work[:, 2048:3072].rearrange("p (s n) -> p s n", s=2)
    otok = work[:, 3072:4096].rearrange("p (s n) -> p s n", s=2)
    AD = 4096
    qT = work[:, AD:AD + 2048].rearrange("p (c n) -> p c n", c=4)
    kT = work[:, AD + 2048:AD + 4096].rearrange("p (c n) -> p c n", c=4)
    vB = work[:, AD + 4096:AD + 6144].rearrange("p (t n) -> p t n", t=4)
    oC = work[:, AD + 6144:AD + 12288].rearrange("p (j t n) -> p j t n", j=3, t=4)
    qD = work[:, AD:AD + 4096].rearrange("p (h n) -> p h n", h=8)
    kD = work[:, AD + 4096:AD + 8192].rearrange("p (h n) -> p h n", h=8)
    vD = work[:, AD + 8192:AD + 10240].rearrange("p (t n) -> p t n", t=4)
    vA = work[:, AD + 10240:AD + 10752].rearrange("p (t n) -> p t n", t=4)
    kA = work[:, AD + 10752:AD + 11776].rearrange("p (g n) -> p g n", g=2)
    oN = work[:, AD + 12288:AD + 14336].rearrange("p (t n) -> p t n", t=4)
    merged = work[:, AD + 11776:AD + 15872].rearrange("p (c n) -> p c n", c=8)
    x_sb = work[:, AD:AD + 4096].rearrange("p (t n) -> p t n", t=4)
    h_sb = work[:, AD + 4096:AD + 8192].rearrange("p (t n) -> p t n", t=4)
    hid = work[:, AD + 4096:AD + 6144].rearrange("p (m n) -> p m n", m=4)
    act_e = work[:, AD + 6144:AD + 7168].rearrange("p (m n) -> p m n",
                                                   m=2)
    lam_in = work[:, AD + 8192:AD + 9216].rearrange("p (v n) -> p v n", v=4)
    gates = work[:, AD + 6144:AD + 8192].rearrange("p (t n) -> p t n", t=4)
    oB = gates
    trig_angle, trig_abs = work[:, 1600:1664], work[:, 1664:1728]
    rope_tmp = work[:, 3072:3584]

    bank = [ctx.enter_context(nc.psum_tensor(f"bank{i}", [P, 512], F32)) for i in range(8)]
    PJ = bank[0:4]
    SB = bank[4:6]
    OB = bank[2:4]
    TP = bank[6:8]

    x_keep = nc.dram_tensor("x_keep", (SEQ, DM), F32).ap()
    c0_keep = nc.dram_tensor("c0_keep", (SEQ, BW), F32).ap()
    c0_stats = nc.dram_tensor("c0_stats", (2, SEQ, 8), F32).ap()

    raw_landed = [signal("raw_landed0", unit=16), signal("raw_landed1", unit=16)]
    hi_split = signal("hi_split")
    tile_split = signal("tile_split", before=2)
    tile_used = signal("tile_used", before=1)
    pj_ready = signal("pj_ready", before=1)
    pj_act = signal("pj_act")
    pj_dve = signal("pj_dve", before=8)
    sq_used = signal("sq_used")
    normed = signal("normed")
    tp_ready = signal("tp_ready")
    tp_act = signal("tp_act", before=2)
    tp_dve = signal("tp_dve", before=2)
    s_ready = signal("s_ready")
    s_biased = signal("s_biased", before=1)
    p_ready = signal("p_ready")
    o_ready = signal("o_ready")
    o_out = signal("o_out")
    gains_in = signal("gains_in")
    ssum = signal("ssum")
    lam_dot = signal("lam_dot")
    lam_exp = signal("lam_exp")
    c_diff = signal("c_diff")
    c_exp = signal("c_exp")
    merged_sum = signal("merged_sum")
    merged_hi = signal("merged_hi")
    merged_lo = signal("merged_lo")
    conv_mid = signal("conv_mid")
    e_ready = signal("e_ready")
    hidden_val = signal("hidden_val")
    hidden_hi = signal("hidden_hi")
    hidden_lo = signal("hidden_lo")
    act_step = signal("act_step", before=1)
    dve_step = signal("dve_step", before=1)
    params_in = signal("params_in", before=16, unit=16)
    direct_in = signal("direct_in", unit=16)
    x_moved = signal("x_moved", unit=16)
    c0_moved = signal("c0_moved", unit=16)
    small_in = sem("small_in")
    setup_in = sem("setup_in")
    setup_act = sem("setup_act")
    setup_dve = sem("setup_dve")
    dve_setup = sem("dve_setup")
    x_in = sem("x_in")
    out_done = sem("out_done")
    waits_met = sem("waits_met")
    rows_clear = sem("rows_clear")

    nc.disable_value_cache = True

    def layers(eng):
        return eng.Fori(0, DEPTH)

    def weight_tiles(l):
        def chunk_rows(w, kt, chunks=2):
            return w[bass.ds(l, 1), kt * P * chunks:(kt + 1) * P * chunks, :].rearrange("a (c p) n -> p (a c) n", p=P)

        w_in, w_up, w_down = io["w_in"], io["ffn_w_up"], io["ffn_w_down"]
        w_br = io["w_branch"].rearrange("l b k n -> l (b k) n")

        def block(w, *cols, kts=range(4)):
            for kt in kts:
                at, pieces = 0, []
                for c0, n in cols:
                    pieces.append((at, n, chunk_rows(w, kt)[:, :, c0:c0 + n]))
                    at += n
                yield pieces, 2, at, kt == kts[-1]

        def gate(i, cb):
            yield from block(w_in, (COL["gate"] + i * DM + cb * BW, BW))

        def branch(i, cb):
            yield from block(w_br, (cb * BW, BW), kts=range(2 * i, 2 * i + 2))

        def gate_and_branch(i):
            for cb in range(2):
                yield from gate(i, cb)
                yield from branch(i, cb)

        def d_up(w, hb):
            if w == "q":
                yield [(0, QR, chunk_rows(io["d_w_uq"], 0, 3)[:, :, hb * 384:hb * 384 + 384])], 3, 384, True
            else:
                yield from block(io["d_w_ukv"], (hb * BW, BW), kts=range(1))

        for b in range(9):
            yield from block(w_in, (COL["C"] + b * BW, BW))
        yield from block(w_in, (COL["Akv"], 256), (COL["ckv"], KVR))
        yield from block(w_in, (COL["cq"], QR), (COL["kr"], ROPE))
        yield from gate(2, 0)
        yield from d_up("q", 0)
        yield from branch(2, 0)
        yield from d_up("q", 1)
        yield from gate(2, 1)
        yield from d_up("kv", 0)
        yield from branch(2, 1)
        yield from d_up("kv", 1)
        yield from block(w_in, (COL["Aq"], BW))
        yield from gate_and_branch(3)
        for b in range(3):
            yield from block(w_in, (COL["B"] + b * BW, BW))
        yield from gate_and_branch(0)
        yield from gate_and_branch(1)
        for cb in range(2):
            yield from block(io["w_o"], (cb * BW, BW))
        first = 0
        for n in UP_GROUPS:
            for b in range(first, first + n):
                yield from block(w_up, (256 * b, 256), (FF + 256 * b, 256))
            for cb in range(2):
                yield from block(w_down, (cb * BW, BW), kts=range(first, first + n))
            first += n

    def all_keys(u):
        return 0, TT, TT // 2

    def near_keys(u):
        t = u // 8
        reach = -(-max(A_RADIUS, C_PATTERNS[0][0] // 2) // P)
        lo, hi = max(0, t - reach), min(TT, t + reach + 1)
        return lo, hi, (lo + hi + 1) // 2

    def parameter_rows(layer):
        at = bass.ds(layer, 1)
        for name, key in (("norm1_g", "norm1"), ("norm2_g", "norm2"), ("d_cq_norm", "cq"), ("d_ckv_norm", "ckv"),
                          ("b_subln_g", "subln")):
            src = io[name][at].rearrange("a (r c) -> (a r) c", c=P)
            yield rows[ROW[key]:ROW[key] + src.shape[0], 0, :], src
        for name, key in (("a_q_norm", "aq"), ("a_k_norm", "ak"), ("b_q_norm", "bq"), ("b_k_norm", "bk"),
                          ("c_q_norm", "cqn"), ("c_k_norm", "ckn")):
            yield (rows[ROW[key]:ROW[key] + 1, 0, :].rearrange("p (a n) -> p a n", a=2),
                   io[name][at, :].unsqueeze(1).to_broadcast([1, 2, HD]))
        yield rows[ROW["dq"]:ROW["dq"] + 1, 0, 0:NOPE], io["d_q_norm"][at, 0:NOPE]
        yield rows[ROW["dk"]:ROW["dk"] + 1, 0, 0:NOPE], io["d_k_norm"][at, 0:NOPE]
        conv_w = io["ffn_conv_w"][at].rearrange("a k (r c) -> (a k r) c", c=P)
        yield rows[0:88, 1, :], conv_w[0:88, :]
        yield rows[0:44, 2, :], conv_w[88:132, :]
        yield rows[44:88, 2, :], io["ffn_conv_b"][at].rearrange("a (r c) -> (a r) c", c=P)

    def norm_bank(g0, c):
        return (TP[g0 % 2], TP[(g0 + 1) % 2], SB[0], SB[1])[c % 4]

    block_ = ctx.enter_context(nc.Block())

    @block_.sync
    def _(sp):
        for dst, src in ((work[:, 512:1024].bitcast(I32), io["positions"][0, :].partition_broadcast(P)),
                         (work[:, 256:260].bitcast(I32), io["positions"].rearrange("a (t p) -> p (a t)", p=P)),
                         (work[:, 260:264].bitcast(I32), io["positions"].rearrange("a (p r) -> p (a r)", r=RES)),
                         (consts[:], io["k_consts"])):
            sp.dma_start(dst, src, allow_slow_non_contiguous=True).then_inc(small_in, 16)
        sp.dma_start(x_sb, io["x"].rearrange("a (t p) n -> p (a t) n", p=P)).then_inc(x_in, 16)
        sp.wait_ge(rows_clear, 1)
        for dst, src in list(parameter_rows(0))[6:]:
            sp.dma_start(dst, src, allow_slow_non_contiguous=True).then_inc(params_in.handle, params_in.unit)
        for dst, src in ((bias_a, io["k_mask_a"]), (bias_c0, io["k_mask_c0"]),
                         (work[:, 0:256].rearrange("p (m n) -> p m n", m=2), io["k_mask_c12"])):
            sp.dma_start(dst, src).then_inc(setup_in, 16)
        with layers(sp) as l:
            for k, (pieces, chunks, cols, _last) in enumerate(weight_tiles(l)):
                sp.wait_ge(*tile_split.at(l, k - 1))
                dst = raw[:, k % 2, 0:chunks * cols].rearrange("p (c n) -> p c n", c=chunks)
                for at, n, src in pieces:
                    sp.dma_start(dst[:, :, at:at + n], src).then_inc(*(raw_landed[k % 2]).up())
        sp.wait_ge(*pj_dve.at(DEPTH, 0))
        sp.dma_start(io["y"].rearrange("a (t p) n -> p (a t) n", p=P), x_sb).then_inc(out_done, 16)
        sp.wait_ge(out_done, 16)

    @block_.gpsimd
    def _(pool):
        for s in (tile_split, tile_used, pj_ready, pj_dve, tp_act, tp_dve, s_biased, act_step, dve_step):
            pool.sem_inc(s.handle, s.before)
        pool.memset(rows[:], 1.0).then_inc(rows_clear, 1)
        pool.memset(one[:], 1.0).then_inc(rows_clear, 1)
        pool.wait_ge(rows_clear, 2)
        with layers(pool) as l:
            landed = [0, 0]
            released = [(tile_used, 0), (pj_ready, 0)]
            used = ready = 0
            for k, (pieces, chunks, cols, last) in enumerate(weight_tiles(l)):
                s, n = k % 2, chunks * cols
                landed[s] += len(pieces)
                pool.wait_ge(*raw_landed[s].at(l, landed[s]))
                user, count = released[k]
                pool.wait_ge(*user.at(l, count))
                src = raw[:, s, 0:n]
                pool.tensor_tensor(wh[:, s, 0:n], src, one[:].to_broadcast([P, n]), ALU.mult).then_inc(*hi_split.up())
                pool.wait_ge(*hi_split.at(l, hi_split.n))
                pool.tensor_tensor(wl[:, s, 0:n], src, wh[:, s, 0:n].bitcast(F32),
                                   ALU.subtract).then_inc(*tile_split.up())
                if last:
                    ready += 4
                else:
                    used += 1
                released.append((pj_ready, ready) if last else (tile_used, used))

    @block_.tensor
    def _(pe):
        mm = nc.tensor.matmul
        pe.wait_ge(small_in, 16 * 4)

        with layers(pe) as l:
            n_tile, n_group, n_unit, n_normed = [0], [0], [0], [0]
            taken = {pj_act: 0, pj_dve: 0}
            holder = [(pj_dve, b - 3) for b in range(4)]

            def split3(out, stationary, moving, start, stop):
                mm(out, stationary[0], moving[0], start=start, stop=False)
                mm(out, stationary[0], moving[1], start=False, stop=False)
                return mm(out, stationary[1], moving[0], start=False, stop=stop)

            def block(ntiles, operands, by, chunks=2, cols=512, width=512, hooks=(), before=None):
                step = 0
                for i in range(ntiles):
                    s = n_tile[0] % 2
                    pe.wait_ge(*tile_split.at(l, n_tile[0] + 1))
                    w = [t[:, s, 0:chunks * cols].rearrange("p (c n) -> p c n", c=chunks) for t in (wh, wl)]
                    for b in range(4):
                        if i == 0:
                            taker, count = holder[b]
                            pe.wait_ge(*taker.at(l, count))
                            taken[by] += 1
                            holder[b] = (by, taken[by])
                        if before is not None:
                            before(i, b)
                        for c in range(chunks):
                            st, mv = operands(b, chunks * i + c, [t[:, c, :] for t in w])
                            last = split3(PJ[b][:, 0:width], st, mv, i == 0 and c == 0,
                                          i == ntiles - 1 and c == chunks - 1)
                        if i == ntiles - 1:
                            last.then_inc(*pj_ready.up())
                        elif b == 3:
                            last.then_inc(*tile_used.up())
                        step += 1
                        for after, between in hooks:
                            if after == step:
                                between()
                    n_tile[0] += 1

            def tokens_out(act, first=0, perm=False):
                def operands(b, kc, w):
                    views = [a[:, first + kc, :] for a in act]
                    if perm:
                        views = [v.rearrange("p (i r) -> p r i", r=RES)[:, b, :] for v in views]
                    else:
                        views = [v[:, P * b:P * b + P] for v in views]
                    return views, w
                return operands

            def features_out(act, first=0):
                def operands(b, kc, w):
                    return [t[:, P * b:P * b + P] for t in w], [a[:, first + kc, :] for a in act]
                return operands

            H, G = (hTh, hTl), (gTh, gTl)

            def transposes(sources, at=0):
                g = n_group[0]
                pe.wait_ge(*tp_act.at(l, g - 1))
                pe.wait_ge(*tp_dve.at(l, g - 1))
                for n, src in enumerate(sources, at):
                    k, m = src.shape[0], src.shape[1]
                    last = nc.tensor.transpose(TP[g % 2][0:m, n * P:n * P + k], src, ident[0:k, 0:k])
                n_group[0] += 1
                last.then_inc(*tp_ready.up())

            def norm_transposes():
                n_normed[0] += 4
                pe.wait_ge(*normed.at(l, n_normed[0]))
                g0 = n_group[0]
                for c in range(DC):
                    g = n_group[0]
                    if c < 2:
                        pe.wait_ge(*tp_act.at(l, g - 1))
                        pe.wait_ge(*tp_dve.at(l, g - 1))
                    elif c < 4:
                        pe.wait_ge(*s_biased.at(l, n_unit[0]))
                    else:
                        pe.wait_ge(*tp_act.at(l, g - 3))
                        pe.wait_ge(*tp_dve.at(l, g - 3))
                    dst = norm_bank(g0, c)
                    for t in range(4):
                        last = nc.tensor.transpose(dst[:, t * P:t * P + P], h_sb[:, t, P * c:P * c + P], ident)
                    n_group[0] += 1
                    last.then_inc(*tp_ready.up())

                def chunks_out(i, b):
                    if b == 0:
                        pe.wait_ge(*tp_act.at(l, g0 + 2 * i + 2))
                        pe.wait_ge(*tp_dve.at(l, g0 + 2 * i + 2))
                return chunks_out

            def normed_transposes(sources):
                n_normed[0] += 1
                pe.wait_ge(*normed.at(l, n_normed[0]))
                transposes(sources)

            def transposed_out():
                pe.wait_ge(*tp_act.at(l, n_group[0]))
                pe.wait_ge(*tp_dve.at(l, n_group[0]))

            def hook_groups(make, at=(7, 9, 11, 13)):
                return [(at[t], lambda t=t: normed_transposes(make(t))) for t in range(4)]

            def score(u, scores_of):
                for out, st, mv in scores_of(u, SB[u % 2]):
                    last = mm(out, st, mv, start=True, stop=True)
                last.then_inc(*s_ready.up())

            def first_scores(scores_of, at):
                def start(u):
                    transposed_out()
                    score(u, scores_of)
                return [(at, lambda: start(0)), (at + 1, lambda: start(1))]

            def attention(n, scores_of, values_of, keys=all_keys, started=0, tile_out=None):
                if not started:
                    transposed_out()
                    pe.wait_ge(*pj_act.at(l, taken[pj_act]))
                first, group = n_unit[0], {}
                for step in range(started, n + 3):
                    if step < n:
                        if step >= 2:
                            pe.wait_ge(*s_biased.at(l, first + step - 1))
                        score(step, scores_of)
                    if 2 <= step < n + 2:
                        u = step - 2
                        pe.wait_ge(*p_ready.at(l, first + u + 1))
                        group[u] = n_group[0]
                        lo, hi, _mid = keys(u)
                        transposes([probs[:, u % 2, P * k:P * k + P] for k in range(lo, hi)], at=lo)
                    if step >= 3:
                        u = step - 3
                        pe.wait_ge(*tp_act.at(l, group[u] + 1))
                        pe.wait_ge(*tp_dve.at(l, group[u] + 1))
                        if u >= 2:
                            pe.wait_ge(*o_out.at(l, first + u - 1))
                        elif started and u == 0:
                            pe.wait_ge(*pj_act.at(l, taken[pj_act]))
                            pe.wait_ge(*pj_dve.at(l, taken[pj_dve]))
                        for out, st, mv, start, stop in values_of(u, OB[u % 2], probsT[:, u % 2, :]):
                            last = mm(out, st, mv, start=start, stop=stop)
                        last.then_inc(*o_ready.up())
                    if tile_out and step >= 12 and (step - 12) % 8 == 0:
                        tile_out((step - 12) // 8)
                n_unit[0] += n
                holder[2] = holder[3] = (o_out, n_unit[0])

            def dense_values(v_of, width, keys=all_keys):
                def values_of(u, out, pt):
                    lo, hi, _mid = keys(u)
                    return [(out[:, 0:width], pt[:, P * k:P * k + P], v_of(u, k), k == lo, k == hi - 1)
                            for k in range(lo, hi)]
                return values_of

            def gate_block(hooks=()):
                block(4, features_out(H), pj_act, hooks=hooks)

            def branch_block(hooks=()):
                transposed_out()
                block(2, features_out(G), pj_dve, hooks=hooks)

            def gates_and_branch(hooks=(), last_hooks=()):
                for cb in range(2):
                    gate_block(hooks if cb == 0 else ())
                    branch_block(last_hooks if cb == 1 else ())

            def q_tile(h, t):
                return qT[64 * (h % 2):64 * (h % 2) + 64, h // 2, P * t:P * t + P]

            def out_tiles(t):
                return [otok[:, t % 2, P * c:P * c + P] for c in range(4)]

            pe.wait_ge(*params_in.at(l, 0))
            transposes([rows[:, n, :] for n in range(3)])
            chunks_out = norm_transposes()

            staged = lambda t: [stage[:, t, P * c:P * c + P] for c in range(4)]
            for j in range(3):
                if j == 0:
                    def scores_of(u, out):
                        lo, hi, _mid = near_keys(u)
                        return [(out[:, P * lo:P * hi], q_tile(u % 8, u // 8),
                                 kT[64 * (u % 2):64 * (u % 2) + 64, (u % 8) // 2, P * lo:P * hi])]
                    values_of = dense_values(lambda u, k: vB[:, k, HD * (u % 8):HD * (u % 8) + HD], HD, near_keys)
                else:
                    scores_of = lambda h, out: [(out[:, P * r:P * r + P], q_tile(h, r),
                                                 kT[64 * (h % 2):64 * (h % 2) + 64, h // 2, P * r:P * r + P])
                                                for r in range(RES)]
                    values_of = lambda h, out, pt: [(out[:, HD * r:HD * r + HD], pt[:, P * r:P * r + P],
                                                     vB[:, r, HD * h:HD * h + HD], True, True) for r in range(RES)]
                block(4, tokens_out(H, perm=j > 0), pj_act, before=chunks_out if j == 0 else None)
                block(4, tokens_out(H, perm=j > 0), pj_act, hooks=hook_groups(staged))
                block(4, tokens_out(H, perm=j > 0), pj_act,
                      hooks=hook_groups(staged, at=(7, 9, 10, 12)) + first_scores(scores_of, 14))
                attention(8 if j else 32, scores_of, values_of, keys=all_keys if j else near_keys, started=2)

            block(4, tokens_out(H), pj_act,
                  hooks=hook_groups(lambda t: [oC[:, 0, t, P * c:P * c + P] for c in range(4)], at=(13, 14, 15, 16)))
            block(4, tokens_out(H), pj_act, cols=416, width=416, hooks=hook_groups(
                lambda t: [kdup[:, t, 0:P], kdup[:, t, P:2 * P], stage[:, t, 256:384], stage[:, t, 384:512]], at=(12,
                        13, 14, 15)))
            gate_block(hook_groups(lambda t: [stage[:, t, P * c:P * c + P] for c in range(3)], at=(10, 11, 12, 13)))
            dq_tiles = lambda t: [stage[:, t, DQK * h:DQK * h + DQK] for h in range(4)]
            dk_tiles = lambda t: [stage[:, t, P * h:P * h + DQK] for h in range(4)]
            transposed_out()
            block(1, tokens_out(G, first=LAT_Q), pj_act, chunks=3, cols=384, width=384)
            branch_block()
            n_normed[0] += 1
            pe.wait_ge(*normed.at(l, n_normed[0]))
            for t in range(4):
                transposes(dq_tiles(t))
            block(1, tokens_out(G, first=LAT_Q), pj_act, chunks=3, cols=384, width=384)
            gate_block([(10, lambda: normed_transposes(dq_tiles(0)))]
                       + [(10 + t, lambda t=t: transposes(dq_tiles(t))) for t in (1, 2, 3)])
            block(1, tokens_out(G, first=LAT_KV), pj_act)
            branch_block()
            for t in range(4):
                normed_transposes(dk_tiles(t))
            block(1, tokens_out(G, first=LAT_KV), pj_act)
            for t in range(4):
                normed_transposes(dk_tiles(t))
            attention(32,
                      lambda u, out: [(out[:], qD[0:DQK, u % 8, P * (u // 8):P * (u // 8) + P], kD[0:DQK, u % 8, :])],
                      dense_values(lambda u, k: vD[:, k, DV * (u % 8):DV * (u % 8) + DV], DV),
                      tile_out=lambda t: normed_transposes(out_tiles(t)))

            last_tile = [(2, lambda: normed_transposes(out_tiles(3)))]
            block(4, tokens_out(H), pj_act, hooks=last_tile)

            def a_scores(u, out):
                lo, hi, _mid = near_keys(u)
                return [(out[:, P * lo:P * hi], q_tile(u % 8, u // 8),
                         kA[64 * (u % 2):64 * (u % 2) + 64, (u % 8) // 4, P * lo:P * hi])]
            gates_and_branch(hook_groups(staged), first_scores(a_scores, 3))
            attention(32, a_scores,
                      dense_values(lambda u, k: vA[:, k, HD * ((u % 8) // 4):HD * ((u % 8) // 4) + HD], HD, near_keys),
                      keys=near_keys, started=2, tile_out=lambda t: normed_transposes(out_tiles(t)))

            block(4, tokens_out(H), pj_act, hooks=last_tile)
            block(4, tokens_out(H), pj_act, hooks=hook_groups(staged))
            block(4, tokens_out(H), pj_act, hooks=hook_groups(staged))

            def b_scores(u, out):
                t, h, m = u // 8, (u % 8) // 2, u % 2
                n = 4 * m + h
                return [(out[:], q_tile(n, t), kT[64 * (n % 2):64 * (n % 2) + 64, n // 2, :])]
            gates_and_branch((), first_scores(b_scores, 3))
            attention(32, b_scores, dense_values(lambda u, k: vB[:, k, P * ((u % 8) // 2):P * ((u % 8) // 2) + P], P),
                      started=2)
            gates_and_branch(hook_groups(lambda t: [oB[:, t, P * c:P * c + P] for c in range(4)], at=(9, 10, 11, 12)))

            for cb in range(2):
                block(4, tokens_out(H), pj_dve,
                      before=lambda i, b: pe.wait_ge(*merged_lo.at(l, 2 * i + 2)) if cb == 0 and b == 0 else None)
            chunks_out = norm_transposes()
            hidden = 0
            for group in UP_GROUPS:
                for b in range(group):
                    block(4, features_out(H), pj_dve, before=chunks_out if hidden == 0 and b == 0 else None)
                for cb in range(2):
                    block(group, tokens_out(G), pj_dve,
                          before=lambda i, b: pe.wait_ge(*hidden_lo.at(l,
                                  hidden + 2 * i + 2)) if cb == 0 and b == 0 else None)
                hidden += 2 * group

    @block_.scalar
    def _(act):
        a = nc.scalar.activation
        act.wait_ge(rows_clear, 1)
        for dst, src in list(parameter_rows(0))[:6]:
            act.dma_start(dst, src, allow_slow_non_contiguous=True).then_inc(params_in.handle, params_in.unit)
        act.wait_ge(setup_dve, 4)
        for t in range(4):
            a(bias_b[:, t, :], work[:, 1024:1536], ACT.Abs, bias=stat[:, 0, t:t + 1]).then_inc(setup_act, 1)
        for r in range(RES):
            a(work[:, 2048 + P * r:2048 + P * r + P], work[:, 1024:1536].rearrange("p (i r) -> p r i", r=RES)[:, r, :],
              ACT.Abs,
              bias=stat[:, 0, 4 + r:5 + r]).then_inc(setup_act, 1)
        a(trig_abs, trig_angle, ACT.Abs).then_inc(setup_act, 1)
        a(trig[:, 0, :, :].rearrange("p t n -> p (t n)"), trig_angle, ACT.Sin).then_inc(setup_act, 1)
        act.wait_ge(setup_dve, 5)
        a(trig[:, 1, :, :].rearrange("p t n -> p (t n)"), trig_abs, ACT.Sin).then_inc(setup_act, 1)
        act.wait_ge(x_in, 16)
        act.wait_ge(rows_clear, 1)
        act.wait_ge(setup_act, 11)

        with layers(act) as l:
            n_ready, n_group, n_unit, n_dve, n_merged, n_sq = [0], [0], [0], [0], [0], [0]
            own = Own(act_step)

            def ready():
                n_ready[0] += 1
                act.wait_ge(*pj_ready.at(l, n_ready[0]))
                return PJ[(n_ready[0] - 1) % 4]

            def group():
                n_group[0] += 1
                act.wait_ge(*tp_ready.at(l, n_group[0]))
                return TP[(n_group[0] - 1) % 2]

            L = bass.ds(l, 1)

            def direct(dst, src):
                act.dma_start(dst, src, allow_slow_non_contiguous=True).then_inc(*direct_in.up())

            keep = x_keep.rearrange("(t p) n -> p t n", p=P)

            def staged_squares(width, extra=None, view=lambda s: s, before=None):
                for t in range(4):
                    if before is not None:
                        before(t)
                    src = ready()
                    if extra is not None:
                        a(*extra(t, src), ACT.Copy).then_inc(*act_step.up(own))
                    if n_sq[0] >= 2:
                        act.wait_ge(*sq_used.at(l, n_sq[0] - 1))
                    a(view(sq[:, n_sq[0] % 2, 0:width]), view(src[:, 0:width]), ACT.Square).then_inc(*act_step.up(own))
                    n_sq[0] += 1
                    a(stage[:, t, 0:width], src[:, 0:width], ACT.Copy).then_inc(*pj_act.up(own))

            def half_out(dst, gain_of=None, same=None, m=P):
                src = group()
                if same is not None:
                    a(dst(0, 2), src[0:m, 0:2 * P].rearrange("p (c n) -> p c n", c=2), ACT.Copy,
                      scale=same).then_inc(*tp_act.up(own))
                else:
                    for c in range(2):
                            a(dst(c, c + 1), src[0:m, P * c:P * c + P].unsqueeze(1), ACT.Copy,
                              scale=gain_of(c)).then_inc(*(tp_act if c else act_step).up(own))

            def hi_out(dst, gain_col=None):
                kw = {} if gain_col is None else dict(scale=gain_col)
                src = group()
                act.wait_ge(*own.done(l))
                a(dst, src[:, :].rearrange("p (c n) -> p c n", c=4), ACT.Copy, **kw).then_inc(*tp_act.up(own))

            def squares(added):
                for half in range(2):
                    for t in range(4):
                        act.wait_ge(*pj_dve.at(l, added + 4 * half + t + 1))
                        cols = slice(BW * half, BW * half + BW)
                        act.wait_ge(*own.done(l))
                        a(h_sb[:, t, cols], x_sb[:, t, cols], ACT.Square,
                          accum_out=stat[:, 0, 4 * half + t:4 * half + t + 1]).then_inc(*ssum.up(own))

            def norm_out(row):
                g0 = n_group[0]
                for c in range(DC):
                    group()
                    act.wait_ge(*own.done(l))
                    a(hTh[:, c, :], norm_bank(g0, c)[:, :], ACT.Copy,
                      scale=prm[:, row + c:row + c + 1]).then_inc(*tp_act.up(own))

            def exps(u, subs=1, mins=5, sums=8, with_sink=False, keys=all_keys):
                lo, hi, _mid = keys(u)
                act.wait_ge(*s_biased.at(l, n_unit[0] + u + 1))
                if with_sink:
                    a(stat[:, 11, u:u + 1], sink[:, u % 8:u % 8 + 1], ACT.Exp, scale=-1.0,
                      bias=stat[:, 5, u:u + 1]).then_inc(*act_step.up(own))
                w = P * (hi - lo) // subs
                for r in range(subs):
                    c = u if subs == 1 else 8 * r + u
                    at = P * lo + w * r
                    a(probs[:, u % 2, at:at + w], scores[:, u % 2, at:at + w], ACT.Exp, scale=-1.0,
                      bias=stat[:, mins, c:c + 1],
                      accum_out=stat[:, sums, c:c + 1]).then_inc(*(p_ready if r == subs - 1 else act_step).up(own))

            def attention(n, started=0, tile_out=None, keys=all_keys, **kw):
                first = n_unit[0]
                for step in range(started, n + 3):
                    if 2 <= step < n + 2:
                        u = step - 2
                        lo, _hi, mid = keys(u)
                        src = group()
                        if u >= 2:
                            act.wait_ge(*o_ready.at(l, first + u - 1))
                        a(probsT[:, u % 2, P * lo:P * mid], src[:, P * lo:P * mid], ACT.Copy).then_inc(*tp_act.up(own))
                    if step < n:
                        exps(step, keys=keys, **kw)
                    if tile_out and step >= 12 and (step - 12) % 8 == 0:
                        tile_out((step - 12) // 8)
                n_unit[0] += n

            def gates_out():
                if n_merged[0]:
                    act.wait_ge(*merged_sum.at(l, n_merged[0]))
                else:
                    act.wait_ge(*pj_dve.at(l, n_dve[0]))
                for m in range(4):
                    src = ready()
                    act.wait_ge(*own.done(l))
                    a(gates[:, m, :], src[:, :], ACT.Tanh, scale=0.5).then_inc(*pj_act.up(own))

            def branch_skipped():
                n_ready[0] += 4
                n_dve[0] += 4

            def gates_and_branch(order, start=lambda: None):
                for cb in range(2):
                    gates_out()
                    if cb == 1:
                        start()
                    elif order == 1:
                        for dst, src in parameter_rows((DEPTH - 1) - l):
                            act.dma_start(dst, src, allow_slow_non_contiguous=True).then_inc(*params_in.up())
                    branch_skipped()
                    n_merged[0] += 4

            def oT(t):
                return gTh[:, 0:4, P * t:P * t + P]

            squares(-8)
            src = group()
            act.wait_ge(*own.done(l))
            a(prm[:, 0:NROW], src[:, 0:NROW], ACT.Copy).then_inc(*act_step.up(own))
            act.wait_ge(*own.done(l))
            a(prm[:, NROW:NROW + 88], src[:, P:P + 88], ACT.Copy).then_inc(*tp_act.up(own))
            norm_out(ROW["norm1"])
            act.dma_start(keep, x_sb).then_inc(*x_moved.up())
            for n, name in enumerate(("d_q_norm", "d_k_norm")):
                direct(rope_rows[:, n, :], io[name][L, NOPE:DQK].broadcast_to([P, ROPE]))
            direct(sink[:], io["a_sink"][L, :].broadcast_to([P, 8]))
            direct(lamc[:], io["k_lam"][L, :].broadcast_to([P, 2]))
            for n, name in enumerate(("b_lam_q1", "b_lam_k1", "b_lam_q2", "b_lam_k2")):
                direct(lam_in[:, n, :], io[name][L].rearrange("a h n -> a (h n)").broadcast_to([P, 256]))
            for j in range(3):
                staged_squares(512)
                if j == 0:
                    act.wait_ge(*x_moved.at(l, 1))
                    act.wait_ge(*gains_in.at(l, 1))
                if j == 1:
                    act.wait_ge(*o_out.at(l, 32))
                    act.dma_start(c0_keep.rearrange("(t p) n -> p t n", p=P), oN).then_inc(*c0_moved.up())
                    for n in range(2):
                        act.dma_start(c0_stats[n].rearrange("(t p) h -> p t h", p=P),
                                      stat[:, 12 + n, :].rearrange("p (t h) -> p t h", t=4)).then_inc(*c0_moved.up())
                for t in range(4):
                    half_out(lambda c0, c1: qT[:, c0:c1, P * t:P * t + P],
                             lambda c: gain[:, 8 + 4 * j + c:9 + 4 * j + c])
                if j == 0:
                    act.wait_ge(*lam_dot.at(l, 1))
                    act.wait_ge(*own.done(l))
                    a(lam[:], lam[:], ACT.Exp).then_inc(*lam_exp.up(own))
                staged_squares(512)
                if j == 1:
                    act.wait_ge(*c0_moved.at(l, 3))
                    act.dma_start(oC[:, 0, :, :], c0_keep.rearrange("(p r) n -> p r n", r=RES)).then_inc(*c0_moved.up())
                    for n in range(2):
                        act.dma_start(stat[:, 5 + 3 * n, :].rearrange("p (r h) -> p r h", r=RES),
                                      c0_stats[n].rearrange("(p r) h -> p r h", r=RES)).then_inc(*c0_moved.up())
                for t in range(4):
                    half_out(lambda c0, c1: kT[:, c0:c1, P * t:P * t + P], same=prm[:, ROW["ckn"]:ROW["ckn"] + 1])
                kw = dict(subs=4, mins=5 + j, sums=8 + j) if j else dict(mins=12, sums=13, keys=near_keys)
                for t in range(4):
                    src = ready()
                    a(vB[:, t, :], src[:, :], ACT.Copy).then_inc(*pj_act.up(own))
                    if t < 2:
                        exps(t, **kw)
                attention(8 if j else 32, started=2, **kw)
            act.wait_ge(*c_diff.at(l, 1))
            act.wait_ge(*own.done(l))
            a(stat[:, 12:15, :], stat[:, 12:15, :], ACT.Exp).then_inc(*c_exp.up(own))

            staged_squares(512, extra=lambda t, src: (vA[:, t, :], src[:, P:2 * P]),
                           before=lambda r: hi_out(gTh[:, 0:4, :].rearrange("p c (i r) -> p r c i", r=RES)[:, r]))
            for t in range(4):
                src = group()
                act.wait_ge(*own.done(l))
                a(kA[:, :, P * t:P * t + P], src[:, 0:256].rearrange("p (c n) -> p c n", c=2), ACT.Copy,
                  scale=prm[:, ROW["ak"]:ROW["ak"] + 1]).then_inc(*act_step.up(own))
                for c in range(2):
                    act.wait_ge(*own.done(l))
                    a(gTh[:, LAT_KV + c, P * t:P * t + P], src[:, 256 + P * c:384 + P * c], ACT.Copy,
                      scale=prm[:, ROW["ckv"] + c:ROW["ckv"] + c + 1]).then_inc(*(tp_act if c else act_step).up(own))
            staged_squares(416)
            for t in range(4):
                src = group()
                for c in range(3):
                    act.wait_ge(*own.done(l))
                    a(gTh[:, LAT_Q + c, P * t:P * t + P], src[:, P * c:P * c + P], ACT.Copy,
                      scale=prm[:, ROW["cq"] + c:ROW["cq"] + c + 1]).then_inc(*(tp_act if c == 2 else act_step).up(own))
            gates_out()
            for hb in range(2):
                staged_squares(384)
                if hb == 0:
                    branch_skipped()
                for t in range(4):
                    half_out(lambda c0, c1: qD[0:DQK, 4 * hb + c0:4 * hb + c1, P * t:P * t + P],
                             same=gain[0:DQK, 21:22], m=DQK)
            gates_out()
            for hb in range(2):
                staged_squares(512, extra=lambda t, src: (
                    vD[:, t, 256 * hb:256 * hb + 256].rearrange("p (h n) -> p h n", h=4),
                    src[:, :].rearrange("p (h n) -> p h n", h=4)[:, :, NOPE:P]),
                    view=lambda s: s.rearrange("p (h n) -> p h n", h=4)[:, :, 0:NOPE])
                if hb == 0:
                    branch_skipped()
                for t in range(4):
                    half_out(lambda c0, c1: kD[0:DQK, 4 * hb + c0:4 * hb + c1, P * t:P * t + P],
                             same=prm[0:DQK, ROW["dk"]:ROW["dk"] + 1], m=DQK)
            attention(32, tile_out=lambda t: hi_out(oT(t)))
            hi_out(oT(3))

            staged_squares(512)
            for t in range(4):
                half_out(lambda c0, c1: qT[:, c0:c1, P * t:P * t + P], lambda c: gain[:, c:c + 1])
            kw = dict(with_sink=True, keys=near_keys)
            gates_and_branch(1, lambda: [exps(u, **kw) for u in range(2)])
            attention(32, started=2, tile_out=lambda t: hi_out(oT(t)), **kw)
            hi_out(oT(3))

            staged_squares(512)
            for t in range(4):
                half_out(lambda c0, c1: qT[:, c0:c1, P * t:P * t + P], lambda c: gain[:, 4 + c:5 + c])
            staged_squares(512)
            for t in range(4):
                half_out(lambda c0, c1: kT[:, c0:c1, P * t:P * t + P], same=prm[:, ROW["bk"]:ROW["bk"] + 1])
            for t in range(4):
                src = ready()
                a(vB[:, t, :], src[:, :], ACT.Copy).then_inc(*pj_act.up(own))
            gates_and_branch(2, lambda: [exps(u) for u in range(2)])
            attention(32, started=2)
            act.wait_ge(*o_ready.at(l, n_unit[0]))
            act.wait_ge(*x_moved.at(l, 1))
            act.dma_start(x_sb, keep).then_inc(*x_moved.up())
            for t in range(4):
                hi_out(oT(t), gain[:, 20:21])
            gates_and_branch(3)

            for c in range(DC):
                act.wait_ge(*merged_sum.at(l, 16 + c + 1))
                act.wait_ge(*own.done(l))
                a(hTh[:, c, :], merged[:, c, :], ACT.Copy, scale=0.5).then_inc(*merged_hi.up(own))
            n_ready[0] += 8
            squares(n_dve[0])
            norm_out(ROW["norm2"])
            n_dve[0] += 8

            b = 0
            for size in UP_GROUPS:
                for i in range(size):
                    for m in range(4):
                        src = ready()
                        if m == 0 and b > 0:
                            act.wait_ge(*hidden_lo.at(l, 2 * b))
                        q = 2 * b + m if m < 2 else CONV_B // 2 + 2 * b + m - 2
                        act.wait_ge(*own.done(l))
                        a(hid[:, m, :], src[:, :], ACT.Identity, scale=prm[:, NROW + 44 + q:NROW + 45 + q],
                          bias=prm[:, NROW + 132 + q:NROW + 133 + q]).then_inc(*conv_mid.up(own))
                    for m in range(2):
                        act.wait_ge(*pj_dve.at(l, n_dve[0] + m + 1))
                        act.wait_ge(*own.done(l))
                        a(act_e[:, m, :], hid[:, m, :], ACT.Tanh, scale=0.5).then_inc(*e_ready.up(own))
                    n_dve[0] += 4
                    for m in range(2):
                        act.wait_ge(*hidden_val.at(l, 2 * b + m + 1))
                        act.wait_ge(*own.done(l))
                        a(gTh[:, 2 * i + m, :], act_e[:, m, :], ACT.Copy, scale=0.5).then_inc(*hidden_hi.up(own))
                    b += 1
                n_dve[0] += 8
                n_ready[0] += 8
        act.wait_ge(*params_in.at(DEPTH, 0))

    @block_.vector
    def _(dve):
        v = nc.vector
        setup = [0, 0]

        def su(ins):
            setup[0] += 1
            ins.then_inc(dve_setup, 1)
            dve.wait_ge(dve_setup, setup[0])

        def publish():
            setup[1] += 1
            v.tensor_copy(lamc[:, 0:1], stat[:, 15, 0:1]).then_inc(setup_dve, 1)
            dve.wait_ge(setup_dve, setup[1])

        dve.wait_ge(small_in, 16 * 4)
        su(v.memset(stat[:], 0.0))
        su(v.tensor_copy(work[:, 1024:1536], work[:, 512:1024].bitcast(I32)))
        su(v.tensor_copy(stat[:, 1, 0:8], work[:, 256:264].bitcast(I32)))
        su(v.tensor_scalar(stat[:, 0, 0:8], stat[:, 1, 0:8], -1.0, None, ALU.mult))
        for t in range(4):
            su(v.tensor_scalar(trig_angle[:, 16 * t:16 * t + 16], consts[:, 148:164], stat[:, 1, t:t + 1], None,
                               ALU.mult))
        turns = work[:, 1536:1600]
        su(v.tensor_scalar(turns, trig_angle, 1.0 / (2 * math.pi), 12582912.0, ALU.mult, ALU.add))
        su(v.tensor_scalar(turns, turns, 12582912.0, None, ALU.subtract))
        c1 = 6.28125
        c2 = float(np.float32(math.floor((2 * math.pi - c1) * 2 ** 17) / 2 ** 17))
        for c in (c1, c2, 2 * math.pi - c1 - c2):
            su(v.scalar_tensor_tensor(trig_angle, turns, -c, trig_angle, ALU.mult, ALU.add))
        su(v.tensor_scalar(trig_angle, trig_angle, 3.1415925, -3.1415925, ALU.min, ALU.max))
        for _i in range(4):
            publish()
        dve.wait_ge(setup_act, 9)
        su(v.tensor_scalar(trig_abs, trig_abs, -1.0, math.pi / 2, ALU.mult, ALU.add))
        publish()
        dve.wait_ge(setup_in, 16 * 3)
        su(v.tensor_tensor(bias_a, bias_a, bias_b, ALU.add))
        su(v.tensor_tensor(bias_c0, bias_c0, bias_b, ALU.add))
        dist = work[:, 2048:2560].rearrange("p (r n) -> p r n", r=4)
        for n in range(2):
            su(v.tensor_tensor(bias_c12[:, n, :].rearrange("p (r n) -> p r n", r=4), dist,
                               work[:, P * n:P * n + P].unsqueeze(1).to_broadcast([P, RES, P]), ALU.add))
        dve.wait_ge(x_in, 16)

        with layers(dve) as l:
            n_ready, n_group, n_unit, n_ssum, n_act = [0], [0], [0], [0], [0]
            own = Own(pj_dve)

            def ready():
                n_ready[0] += 1
                dve.wait_ge(*pj_ready.at(l, n_ready[0]))
                return PJ[(n_ready[0] - 1) % 4]

            def group():
                n_group[0] += 1
                dve.wait_ge(*tp_ready.at(l, n_group[0]))
                return TP[(n_group[0] - 1) % 2]

            def rsqrt(n, means):
                mean, y, t = stat[:, 1, 0:n], stat[:, 2, 0:n], stat[:, 3, 0:n]
                for lo, hi, width in means:
                    dve.wait_ge(*own.done(l))
                    v.tensor_scalar(stat[:, 1, lo:hi], stat[:, 0, lo:hi], 1.0 / width, EPS, ALU.mult,
                                    ALU.add).then_inc(*dve_step.up(own))
                dve.wait_ge(*own.done(l))
                v.tensor_scalar(t.bitcast(I32), mean.bitcast(I32), 1, None,
                                ALU.arith_shift_right).then_inc(*dve_step.up(own))
                dve.wait_ge(*own.done(l))
                v.tensor_scalar(y.bitcast(I32), t.bitcast(I32), -1.0, float(0x5f3759df), ALU.mult,
                                ALU.add).then_inc(*dve_step.up(own))
                for _i in range(3):
                    dve.wait_ge(*own.done(l))
                    v.tensor_tensor(t, y, y, ALU.mult).then_inc(*dve_step.up(own))
                    dve.wait_ge(*own.done(l))
                    v.scalar_tensor_tensor(t, t, -0.5, mean, ALU.mult, ALU.mult).then_inc(*dve_step.up(own))
                    dve.wait_ge(*own.done(l))
                    v.scalar_tensor_tensor(y, t, 1.5, y, ALU.add, ALU.mult).then_inc(*dve_step.up(own))

            def sums(outs, before=None):
                for t in range(4):
                    if before is not None:
                        before(t)
                    n_act[0] += 1
                    dve.wait_ge(*pj_act.at(l, n_act[0]))
                    parts = outs(t, sq[:, sq_used.n % 2, :])
                    for k, (dst, src) in enumerate(parts):
                        v.tensor_reduce(dst, src, AXX,
                                        ALU.add).then_inc(*(sq_used if k == len(parts) - 1 else dve_step).up(own))

            def heads(ap, h):
                return ap.rearrange("p (h n) -> p h n", h=h)

            def over(col, n):
                return col.unsqueeze(2).to_broadcast([P, col.shape[1], n])

            def head_norm():
                sums(lambda t, s: [(stat[:, 0, 8 * t:8 * t + 8], heads(s, 8))])
                rsqrt(32, [(0, 32, HD)])
                for t in range(4):
                    if t == 0:
                        dve.wait_ge(*own.done(l))
                    v.tensor_tensor(heads(stage[:, t, :], 8), heads(stage[:, t, :], 8),
                                    over(stat[:, 2, 8 * t:8 * t + 8], HD), ALU.mult).then_inc(*normed.up(own))

            def half_out(dst, gain_of=None, same=None, m=P):
                src = group()
                dve.wait_ge(*tp_act.at(l, n_group[0]))
                if same is not None:
                    v.tensor_scalar(dst(2, 4), src[0:m, 2 * P:4 * P].rearrange("p (c n) -> p c n", c=2), same, None,
                                    ALU.mult).then_inc(*tp_dve.up(own))
                else:
                    for c in (2, 3):
                        v.tensor_scalar(dst(c, c + 1), src[0:m, P * c:P * c + P].unsqueeze(1), gain_of(c), None,
                                        ALU.mult).then_inc(*(tp_dve if c == 3 else dve_step).up(own))

            def lo_out(lo, hi, gain_col=1.0):
                src = group()
                dve.wait_ge(*tp_act.at(l, n_group[0]))
                dve.wait_ge(*own.done(l))
                v.scalar_tensor_tensor(lo, src[:, :].rearrange("p (c n) -> p c n", c=4), gain_col, hi.bitcast(F32),
                                       ALU.mult, ALU.subtract).then_inc(*tp_dve.up(own))

            def normalise():
                dve.wait_ge(*ssum.at(l, n_ssum[0] + 8))
                n_ssum[0] += 8
                dve.wait_ge(*own.done(l))
                v.tensor_tensor(stat[:, 0, 0:4], stat[:, 0, 0:4], stat[:, 0, 4:8], ALU.add).then_inc(*dve_step.up(own))
                rsqrt(4, [(0, 4, DM)])
                for t in range(4):
                    if t == 0:
                        dve.wait_ge(*own.done(l))
                    v.tensor_scalar(h_sb[:, t, :], x_sb[:, t, :], stat[:, 2, t:t + 1], None,
                                    ALU.mult).then_inc(*normed.up(own))

            def norm_out(row):
                g0 = n_group[0]
                for c in range(DC):
                    group()
                    src = norm_bank(g0, c)
                    dve.wait_ge(*tp_act.at(l, n_group[0]))
                    v.scalar_tensor_tensor(hTl[:, c, :], src[:, :], prm[:, row + c:row + c + 1],
                                           hTh[:, c, :].bitcast(F32), ALU.mult, ALU.subtract).then_inc(*tp_dve.up(own))

            def bias_step(u, biased):
                dve.wait_ge(*s_ready.at(l, n_unit[0] + u + 1))
                if u >= 2:
                    dve.wait_ge(*p_ready.at(l, n_unit[0] + u - 1))
                biased(u, SB[u % 2], scores[:, u % 2, :])

            def attention(n, biased, out, started=0, keys=all_keys, tile_out=None, merges=()):
                first = n_unit[0]
                for step in range(started, n + 3):
                    if step < n:
                        bias_step(step, biased)
                    if 2 <= step < n + 2:
                        u = step - 2
                        _lo, hi, mid = keys(u)
                        src = group()
                        if u >= 2:
                            dve.wait_ge(*o_ready.at(l, first + u - 1))
                        dve.wait_ge(*tp_act.at(l, n_group[0]))
                        v.tensor_copy(probsT[:, u % 2, P * mid:P * hi],
                                      src[:, P * mid:P * hi]).then_inc(*tp_dve.up(own))
                    if step >= 3:
                        u = step - 3
                        dve.wait_ge(*o_ready.at(l, first + u + 1))
                        out(u, OB[u % 2][:, 0:256])
                        if u < len(merges):
                            merge(*merges[u])
                    if tile_out and step >= 12 and (step - 12) % 8 == 0:
                        tile_out((step - 12) // 8)
                n_unit[0] += n

            def biased_dense(bias_t, slopes, floor=None, head=lambda u: u % 8, keys=all_keys, mins=5):
                def biased(u, src, dst):
                    lo, hi, _mid = keys(u)
                    cols = slice(P * lo, P * hi)
                    start = MASKED if floor is None else floor(u)
                    dve.sem_inc(waits_met, 1)
                    v.tensor_tensor_reduce(out=dst[:, cols], in0=src[:, cols], in1=bias_t[:, u // 8, cols],
                                           scale=slopes[head(u)], scalar=start, accum_out=stat[:, mins, u:u + 1],
                                           op0=ALU.add, op1=ALU.min).then_inc(*s_biased.up(own))
                return biased

            def keep_outputs(u, src):
                t, h = u // 8, u % 8
                v.tensor_copy(otok[:, t % 2, HD * h:HD * h + HD], src[:, 0:HD]).then_inc(*o_out.up(own))

            def dense_out(with_sink=False):
                def out(u, src):
                    keep_outputs(u, src)
                    if u % 8 < 7:
                        return
                    t = u // 8
                    den = stat[:, 8, 8 * t:8 * t + 8]
                    if with_sink:
                        dve.wait_ge(*own.done(l))
                        v.tensor_tensor(den, den, stat[:, 11, 8 * t:8 * t + 8], ALU.add).then_inc(*dve_step.up(own))
                    dve.wait_ge(*own.done(l))
                    v.reciprocal(stat[:, 4, 16:24], den).then_inc(*dve_step.up(own))
                    o = heads(otok[:, t % 2, :], 8)
                    dve.wait_ge(*own.done(l))
                    v.tensor_tensor(o, o, over(stat[:, 4, 16:24], HD), ALU.mult).then_inc(*normed.up(own))
                return out

            def tile_steps(t, gain_col=1.0):
                lo_out(gTl[:, 0:4, P * t:P * t + P], gTh[:, 0:4, P * t:P * t + P], gain_col)

            def gates_skipped():
                n_ready[0] += 4
                n_act[0] += 4

            def branch_out(order, cb, later=()):
                dve.wait_ge(*pj_act.at(l, n_act[0]))
                for m in range(4):
                    src = ready()
                    dst = merged[:, 4 * cb + m, :] if order == 0 else gates[:, m, :]
                    v.scalar_tensor_tensor(dst, gates[:, m, :], 1.0, src[:, :], ALU.add,
                                           ALU.mult).then_inc(*pj_dve.up(own))
                    if order and m not in later:
                        merge(cb, m)

            def merge(cb, m):
                c = 4 * cb + m
                dve.wait_ge(*own.done(l))
                v.tensor_tensor(merged[:, c, :], merged[:, c, :], gates[:, m, :], ALU.add).then_inc(*merged_sum.up(own))

            def gates_and_branch(order, start=lambda: None):
                for cb in range(2):
                    gates_skipped()
                    if cb == 1:
                        start()
                    if cb == 1 and order == 3:
                        for c in range(4):
                            merged_split(c)
                    branch_out(order, cb, later=(2, 3) if cb == 1 and order < 3 else ())

            def merged_split(c):
                dve.wait_ge(*merged_hi.at(l, c + 1))
                dve.wait_ge(*own.done(l))
                v.scalar_tensor_tensor(hTl[:, c, :], merged[:, c, :], 0.5, hTh[:, c, :].bitcast(F32), ALU.mult,
                                       ALU.subtract).then_inc(*merged_lo.up(own))

            normalise()
            dve.wait_ge(*params_in.at(l, 0))
            src = group()
            dve.wait_ge(*tp_act.at(l, 1))
            dve.wait_ge(*own.done(l))
            v.tensor_copy(prm[:, NROW + 88:NROW + 176], src[:, 256:344]).then_inc(*tp_dve.up(own))
            dve.wait_ge(*tp_act.at(l, 1))
            for at, n, key in ((0, 4, "aq"), (4, 4, "bq"), (8, 12, "cqn")):
                dve.wait_ge(*own.done(l))
                v.tensor_scalar(gain[:, at:at + n], consts[:, 128 + at:128 + at + n], prm[:, ROW[key]:ROW[key] + 1],
                                None, ALU.mult).then_inc(*dve_step.up(own))
            dve.wait_ge(*own.done(l))
            v.tensor_scalar(gain[:, 21:22], prm[:, ROW["dq"]:ROW["dq"] + 1], -DQK ** -0.5, None,
                            ALU.mult).then_inc(*gains_in.up(own))
            norm_out(ROW["norm1"])
            for j in range(3):
                head_norm()
                for t in range(4):
                    if j == 0 and t == 0:
                        dve.wait_ge(*x_moved.at(l, 1))
                    half_out(lambda c0, c1: qT[:, c0:c1, P * t:P * t + P],
                             lambda c: gain[:, 8 + 4 * j + c:9 + 4 * j + c])
                if j == 0:
                    dve.wait_ge(*direct_in.at(l, direct_in.each))
                    dve.wait_ge(*own.done(l))
                    v.tensor_scalar(gain[:, 20:21], prm[:, ROW["subln"]:ROW["subln"] + 1], lamc[:, 1:2], None,
                                    ALU.mult).then_inc(*dve_step.up(own))
                    dve.wait_ge(*own.done(l))
                    v.tensor_scalar(sink[:], sink[:], -1.0, None, ALU.mult).then_inc(*dve_step.up(own))
                    for n in range(2):
                        dve.wait_ge(*own.done(l))
                        v.tensor_tensor(lam_in[:, 2 * n, :], lam_in[:, 2 * n, :], lam_in[:, 2 * n + 1, :],
                                        ALU.mult).then_inc(*dve_step.up(own))
                        dve.wait_ge(*own.done(l))
                        v.tensor_reduce(lam[:, 4 * n:4 * n + 4], heads(lam_in[:, 2 * n, :], 4), AXX,
                                        ALU.add).then_inc(*(lam_dot if n else dve_step).up(own))
                head_norm()
                if j == 0:
                    dve.wait_ge(*lam_exp.at(l, 1))
                    dve.wait_ge(*own.done(l))
                    v.scalar_tensor_tensor(lam[:, 0:4], lam[:, 4:8], lamc[:, 0:1], lam[:, 0:4], ALU.subtract,
                                           ALU.subtract).then_inc(*dve_step.up(own))
                for t in range(4):
                    half_out(lambda c0, c1: kT[:, c0:c1, P * t:P * t + P], same=prm[:, ROW["ckn"]:ROW["ckn"] + 1])
                n_ready[0] += 12
                n_act[0] += 4
                if j == 0:
                    def keep(u, src):
                        v.tensor_copy(oN[:, u // 8, HD * (u % 8):HD * (u % 8) + HD],
                                      src[:, 0:HD]).then_inc(*o_out.up(own))
                    biased = biased_dense(bias_c0, C_SLOPES[0], keys=near_keys, mins=12)
                else:
                    def biased(h, src, dst):
                        for r in range(RES):
                            dve.sem_inc(waits_met, 1)
                            v.tensor_tensor_reduce(out=dst[:, P * r:P * r + P], in0=src[:, P * r:P * r + P],
                                                   in1=bias_c12[:, j - 1, P * r:P * r + P], scale=C_SLOPES[j][h],
                                                   scalar=MASKED, accum_out=stat[:, 5 + j, 8 * r + h:8 * r + h + 1],
                                                   op0=ALU.add,
                                                   op1=ALU.min).then_inc(*(s_biased if r == 3 else dve_step).up(own))

                    def keep(h, src):
                        v.tensor_copy(oC[:, j, :, HD * h:HD * h + HD], heads(src, 4)).then_inc(*o_out.up(own))
                for u in range(2):
                    bias_step(u, biased)
                attention(8 if j else 32, biased, keep, started=2, keys=all_keys if j else near_keys)
            dve.wait_ge(*c0_moved.at(l, 6))
            dve.wait_ge(*own.done(l))
            v.tensor_tensor(stat[:, 15, :], stat[:, 5, :], stat[:, 6, :], ALU.min).then_inc(*dve_step.up(own))
            dve.wait_ge(*own.done(l))
            v.tensor_tensor(stat[:, 15, :], stat[:, 15, :], stat[:, 7, :], ALU.min).then_inc(*dve_step.up(own))
            for j in range(3):
                dve.wait_ge(*own.done(l))
                v.tensor_tensor(stat[:, 12 + j, :], stat[:, 15, :], stat[:, 5 + j, :],
                                ALU.subtract).then_inc(*(c_diff if j == 2 else dve_step).up(own))
            dve.wait_ge(*c_exp.at(l, 1))
            dve.wait_ge(*own.done(l))
            v.tensor_tensor(stat[:, 8:11, :], stat[:, 8:11, :], stat[:, 12:15, :], ALU.mult).then_inc(*dve_step.up(own))
            dve.wait_ge(*own.done(l))
            v.tensor_tensor(stat[:, 8, :], stat[:, 8, :], stat[:, 9, :], ALU.add).then_inc(*dve_step.up(own))
            dve.wait_ge(*own.done(l))
            v.tensor_tensor(stat[:, 8, :], stat[:, 8, :], stat[:, 10, :], ALU.add).then_inc(*dve_step.up(own))
            dve.wait_ge(*own.done(l))
            v.reciprocal(stat[:, 8, :], stat[:, 8, :]).then_inc(*dve_step.up(own))
            for j in range(3):
                dve.wait_ge(*own.done(l))
                v.tensor_tensor(stat[:, 12 + j, :], stat[:, 12 + j, :], stat[:, 8, :],
                                ALU.mult).then_inc(*dve_step.up(own))
            for t in range(4):
                for j in range(3):
                    o = oC[:, j, t, :]
                    dve.wait_ge(*own.done(l))
                    v.tensor_tensor(heads(o, 8), heads(o, 8), over(stat[:, 12 + j, 8 * t:8 * t + 8], HD),
                                    ALU.mult).then_inc(*dve_step.up(own))
                    if j:
                        dve.wait_ge(*own.done(l))
                        v.tensor_tensor(oC[:, 0, t, :], oC[:, 0, t, :], o,
                                        ALU.add).then_inc(*(normed if j == 2 else dve_step).up(own))

            def c_lo_out(r):
                lo_out(gTl[:, 0:4, :].rearrange("p c (i r) -> p r c i", r=RES)[:, r],
                       gTh[:, 0:4, :].rearrange("p c (i r) -> p r c i", r=RES)[:, r])

            sums(lambda t, s: [(stat[:, 0, 2 * t:2 * t + 2], heads(s[:, 0:P], 2)),
                               (stat[:, 0, 8 + t:9 + t], s[:, 256:512])], before=c_lo_out)
            rsqrt(12, [(0, 8, HD), (8, 12, KVR)])
            for t in range(4):
                for dup in range(2):
                    dve.wait_ge(*own.done(l))
                    v.tensor_tensor(kdup[:, t, :].rearrange("p (g d n) -> p g d n", g=2, d=2)[:, :, dup, :],
                                    heads(stage[:, t, 0:P], 2), over(stat[:, 2, 2 * t:2 * t + 2], HD),
                                    ALU.mult).then_inc(*dve_step.up(own))
                dve.wait_ge(*own.done(l))
                v.tensor_scalar(stage[:, t, 256:512], stage[:, t, 256:512], stat[:, 2, 8 + t:9 + t], None,
                                ALU.mult).then_inc(*normed.up(own))
            for t in range(4):
                src = group()
                dve.wait_ge(*tp_act.at(l, n_group[0]))
                for c in range(2):
                    dve.wait_ge(*own.done(l))
                    v.scalar_tensor_tensor(gTl[:, LAT_KV + c, P * t:P * t + P], src[:, 256 + P * c:384 + P * c],
                                           prm[:, ROW["ckv"] + c:ROW["ckv"] + c + 1],
                                           gTh[:, LAT_KV + c, P * t:P * t + P].bitcast(F32), ALU.mult,
                                           ALU.subtract).then_inc(*(tp_dve if c else dve_step).up(own))
            n_ready[0] += 4

            def rope(out1, out2, x1, x2, cos, sin, tmp1, tmp2, last=dve_step):
                tt = v.tensor_tensor
                dve.wait_ge(*own.done(l))
                tt(tmp1, x1, sin, ALU.mult).then_inc(*dve_step.up(own))
                dve.wait_ge(*own.done(l))
                tt(tmp2, x2, sin, ALU.mult).then_inc(*dve_step.up(own))
                dve.wait_ge(*own.done(l))
                tt(x1, x1, cos, ALU.mult).then_inc(*dve_step.up(own))
                dve.wait_ge(*own.done(l))
                tt(x2, x2, cos, ALU.mult).then_inc(*dve_step.up(own))
                dve.wait_ge(*own.done(l))
                tt(out1, x1, tmp2, ALU.subtract).then_inc(*dve_step.up(own))
                dve.wait_ge(*own.done(l))
                tt(out2, x2, tmp1, ALU.add).then_inc(*last.up(own))

            sums(lambda t, s: [(stat[:, 0, t:t + 1], s[:, 0:QR]), (stat[:, 4, 8 + t:9 + t], s[:, QR:QR + ROPE])])
            rsqrt(4, [(0, 4, QR)])
            for t in range(4):
                dve.wait_ge(*own.done(l))
                v.tensor_tensor(krr[:, t, :], stage[:, t, QR:QR + ROPE], rope_rows[:, 1, :],
                                ALU.mult).then_inc(*dve_step.up(own))
                dve.wait_ge(*own.done(l))
                v.tensor_scalar(stage[:, t, 0:QR], stage[:, t, 0:QR], stat[:, 2, t:t + 1], None,
                                ALU.mult).then_inc(*normed.up(own))
            rt = [rope_tmp[:, 64 * n:64 * n + 64].rearrange("p (t n) -> p t n", t=4) for n in range(2)]
            rope(krr[:, :, 0:16], krr[:, :, 16:32], krr[:, :, 0:16], krr[:, :, 16:32], trig[:, 1, :, :],
                 trig[:, 0, :, :], *rt)
            for t in range(4):
                src = group()
                dve.wait_ge(*tp_act.at(l, n_group[0]))
                for c in range(3):
                    dve.wait_ge(*own.done(l))
                    v.scalar_tensor_tensor(gTl[:, LAT_Q + c, P * t:P * t + P], src[:, P * c:P * c + P],
                                           prm[:, ROW["cq"] + c:ROW["cq"] + c + 1],
                                           gTh[:, LAT_Q + c, P * t:P * t + P].bitcast(F32), ALU.mult,
                                           ALU.subtract).then_inc(*(tp_dve if c == 2 else dve_step).up(own))
            n_ready[0] += 4
            gates_skipped()
            for hb in range(2):
                sums(lambda t, s: [(stat[:, 0, 4 * t:4 * t + 4], heads(s[:, 0:384], 4))])
                rsqrt(16, [(0, 16, DQK)])
                for t in range(4):
                    q = heads(stage[:, t, 0:384], 4)
                    if t == 0:
                        dve.wait_ge(*own.done(l))
                    v.tensor_tensor(q, q, over(stat[:, 2, 4 * t:4 * t + 4], DQK), ALU.mult).then_inc(*dve_step.up(own))
                rot = stage[:, :, 0:384].rearrange("p t (h n) -> p t h n", h=4)[:, :, :, NOPE:DQK]
                dve.wait_ge(*own.done(l))
                v.tensor_tensor(rot, rot, rope_rows[:, 0:1, :].unsqueeze(1).to_broadcast([P, 4, 4, ROPE]),
                                ALU.mult).then_inc(*dve_step.up(own))
                cs = [trig[:, n, :, :].unsqueeze(2).to_broadcast([P, 4, 4, 16]) for n in (1, 0)]
                tmp = [rope_tmp[:, 256 * n:256 * n + 256].rearrange("p (t h n) -> p t h n", t=4, h=4) for n in range(2)]
                rope(rot[:, :, :, 0:16], rot[:, :, :, 16:32], rot[:, :, :, 0:16], rot[:, :, :, 16:32], *cs, *tmp,
                     last=normed)
                n_ready[0] += 4
                if hb == 0:
                    branch_out(0, 0)
                for t in range(4):
                    half_out(lambda c0, c1: qD[0:DQK, 4 * hb + c0:4 * hb + c1, P * t:P * t + P],
                             same=gain[0:DQK, 21:22], m=DQK)
            gates_skipped()
            for hb in range(2):
                sums(lambda t, s: [(stat[:, 0, 4 * t:4 * t + 4], heads(s, 4)[:, :, 0:NOPE])])
                total = stat[:, 0, 0:16].rearrange("p (t h) -> p t h", t=4)
                dve.wait_ge(*own.done(l))
                v.tensor_tensor(total, total, over(stat[:, 4, 8:12], 4), ALU.add).then_inc(*dve_step.up(own))
                rsqrt(16, [(0, 16, DQK)])
                for t in range(4):
                    k = heads(stage[:, t, :], 4)
                    if t == 0:
                        dve.wait_ge(*own.done(l))
                    v.tensor_tensor(k[:, :, 0:NOPE], k[:, :, 0:NOPE], over(stat[:, 2, 4 * t:4 * t + 4], NOPE),
                                    ALU.mult).then_inc(*dve_step.up(own))
                    v.tensor_tensor(k[:, :, NOPE:DQK], krr[:, t:t + 1, :].to_broadcast([P, 4, ROPE]),
                                    over(stat[:, 2, 4 * t:4 * t + 4], ROPE), ALU.mult).then_inc(*normed.up(own))
                n_ready[0] += 4
                if hb == 0:
                    branch_out(0, 1)
                for t in range(4):
                    half_out(lambda c0, c1: kD[0:DQK, 4 * hb + c0:4 * hb + c1, P * t:P * t + P],
                             same=prm[0:DQK, ROW["dk"]:ROW["dk"] + 1], m=DQK)

            def biased_d(u, src, dst):
                v.tensor_scalar(dst, src[:, :], 1.0, MASKED, ALU.mult, ALU.min,
                                accum_out=stat[:, 5, u:u + 1]).then_inc(*s_biased.up(own))

            attention(32, biased_d, dense_out(), tile_out=tile_steps)
            tile_steps(3)

            head_norm()
            for t in range(4):
                half_out(lambda c0, c1: qT[:, c0:c1, P * t:P * t + P], lambda c: gain[:, c:c + 1])
            n_ready[0] += 4
            biased = biased_dense(bias_a, A_SLOPES, floor=lambda u: sink[:, u % 8:u % 8 + 1], keys=near_keys)
            gates_and_branch(1, lambda: [bias_step(u, biased) for u in range(2)])
            attention(32, biased, dense_out(with_sink=True), started=2, keys=near_keys, tile_out=tile_steps,
                      merges=((1, 2), (1, 3)))
            tile_steps(3)

            head_norm()
            for t in range(4):
                half_out(lambda c0, c1: qT[:, c0:c1, P * t:P * t + P], lambda c: gain[:, 4 + c:5 + c])
            head_norm()
            for t in range(4):
                half_out(lambda c0, c1: kT[:, c0:c1, P * t:P * t + P], same=prm[:, ROW["bk"]:ROW["bk"] + 1])
            n_ready[0] += 12
            n_act[0] += 4
            biased = biased_dense(bias_b, B_SLOPES, head=lambda u: (u % 8) // 2)
            gates_and_branch(2, lambda: [bias_step(u, biased) for u in range(2)])

            def out_b(u, src):
                t, h, m = u // 8, (u % 8) // 2, u % 2
                o = oB[:, t, P * h:P * h + P]
                dve.wait_ge(*own.done(l))
                v.reciprocal(stat[:, 4, 0:1], stat[:, 8, u:u + 1]).then_inc(*dve_step.up(own))
                if m == 0:
                    dve.wait_ge(*own.done(l))
                    v.tensor_scalar(o, src[:, 0:P], stat[:, 4, 0:1], None, ALU.mult).then_inc(*o_out.up(own))
                else:
                    dve.wait_ge(*own.done(l))
                    v.tensor_tensor(stat[:, 4, 0:1], stat[:, 4, 0:1], lam[:, h:h + 1],
                                    ALU.mult).then_inc(*dve_step.up(own))
                    dve.wait_ge(*own.done(l))
                    v.scalar_tensor_tensor(o, src[:, 0:P], stat[:, 4, 0:1], o, ALU.mult,
                                           ALU.add).then_inc(*o_out.up(own))

            attention(32, biased, out_b, started=2, merges=((1, 2), (1, 3)))
            for t in range(4):
                dve.wait_ge(*own.done(l))
                v.tensor_tensor(sq[:, t % 2, :], oB[:, t, :], oB[:, t, :], ALU.mult).then_inc(*dve_step.up(own))
                dve.wait_ge(*own.done(l))
                v.tensor_reduce(stat[:, 0, 4 * t:4 * t + 4], heads(sq[:, t % 2, :], 4), AXX,
                                ALU.add).then_inc(*dve_step.up(own))
            rsqrt(16, [(0, 16, P)])
            for t in range(4):
                o = heads(oB[:, t, :], 4)
                dve.wait_ge(*own.done(l))
                v.tensor_tensor(o, o, over(stat[:, 2, 4 * t:4 * t + 4], P), ALU.mult).then_inc(*normed.up(own))
            for t in range(4):
                tile_steps(t, gain[:, 20:21])
            gates_and_branch(3)

            for c in range(4, DC):
                merged_split(c)
            dve.wait_ge(*x_moved.at(l, 2))

            def add_to_x():
                for cb in range(2):
                    for t in range(4):
                        src = ready()
                        xs = x_sb[:, t, BW * cb:BW * cb + BW]
                        dve.wait_ge(*own.done(l))
                        v.tensor_tensor(xs, src[:, :], xs, ALU.add).then_inc(*pj_dve.up(own))

            add_to_x()
            normalise()
            norm_out(ROW["norm2"])

            b = 0
            for size in UP_GROUPS:
                for i in range(size):
                    for m in range(4):
                        src = ready()
                        q = 2 * b + m if m < 2 else CONV_B // 2 + 2 * b + m - 2
                        dve.wait_ge(*conv_mid.at(l, 4 * b + m + 1))
                        y = hid[:, m, :]
                        dve.wait_ge(*own.done(l))
                        v.scalar_tensor_tensor(y[:, 1:SEQ], src[:, 0:SEQ - 1], prm[:, NROW + q:NROW + 1 + q],
                                               y[:, 1:SEQ], ALU.mult, ALU.add).then_inc(*dve_step.up(own))
                        dve.wait_ge(*own.done(l))
                        v.scalar_tensor_tensor(y[:, 0:SEQ - 1], src[:, 1:SEQ], prm[:, NROW + 88 + q:NROW + 89 + q],
                                               y[:, 0:SEQ - 1], ALU.mult, ALU.add).then_inc(*pj_dve.up(own))
                    for m in range(2):
                        e = act_e[:, m, :]
                        dve.wait_ge(*e_ready.at(l, 2 * b + m + 1))
                        dve.wait_ge(*own.done(l))
                        v.scalar_tensor_tensor(e, e, 1.0, hid[:, m, :], ALU.add, ALU.mult).then_inc(*dve_step.up(own))
                        dve.wait_ge(*own.done(l))
                        v.tensor_tensor(e, e, hid[:, 2 + m, :], ALU.mult).then_inc(*hidden_val.up(own))
                    for m in range(2):
                        dve.wait_ge(*hidden_hi.at(l, 2 * b + m + 1))
                        dve.wait_ge(*own.done(l))
                        v.scalar_tensor_tensor(gTl[:, 2 * i + m, :], act_e[:, m, :], 0.5,
                                               gTh[:, 2 * i + m, :].bitcast(F32), ALU.mult,
                                               ALU.subtract).then_inc(*hidden_lo.up(own))
                    b += 1
                add_to_x()

    for name, s in signals.items():
        if s.n != s.each:
            wrong[name] = s.n
    assert not wrong, f"increments in a layer: {wrong}"


_INS = ["x", "positions", "norm1_g", "w_in", "a_q_norm", "a_k_norm", "a_sink", "b_q_norm", "b_k_norm", "b_lam_q1",
        "b_lam_k1", "b_lam_q2", "b_lam_k2", "b_subln_g", "c_q_norm", "c_k_norm", "d_cq_norm", "d_ckv_norm", "d_w_uq",
        "d_w_ukv", "d_q_norm", "d_k_norm", "w_branch", "w_o", "norm2_g", "ffn_w_up", "ffn_conv_w", "ffn_conv_b",
        "ffn_w_down"]


def kernel(**inputs):
    import numpy as _np
    import concourse.bacc as _bacc
    from concourse import mybir as _mybir
    from concourse.bass_utils import run_bass_kernel_spmd as _run

    nc = _bacc.Bacc("TRN2", target_bir_lowering=False, num_devices=1)
    arrays, io = {}, {}
    given = {name: _np.ascontiguousarray(inputs[name]) for name in _INS}
    given.update(shape_constants())
    for name, a in given.items():
        arrays[f"in_{name}"] = a
        io[name] = nc.dram_tensor(f"in_{name}", a.shape, _mybir.dt.from_np(a.dtype), kind="ExternalInput").ap()
    io["y"] = nc.dram_tensor("out_y", (1, SEQ, DM), _mybir.dt.from_np(_np.dtype("float32")), kind="ExternalOutput").ap()
    build(nc, io)
    return _run(nc, [arrays], core_ids=[0]).results[0]["out_y"]
```
